# Optimizing a Trainium2 kernel written in Bass

```python
import numpy as np
import jax
import jax.numpy as jnp
from jax import lax

D_MODEL = 1024
BATCH = 1
SEQ = 512
DEPTH = 2

N_MIXERS = 2
RMS_EPS = 1e-6
ROPE_THETA = 10000.0
NEG_INF = -1e30
N_NSA_LAYERS = (DEPTH + 1) // 2
N_MLA_LAYERS = DEPTH // 2

NSA_HEADS = 16
NSA_HEAD_DIM = D_MODEL // NSA_HEADS
NSA_KV_GROUPS = 4
NSA_HEADS_PER_GROUP = NSA_HEADS // NSA_KV_GROUPS
CMP_LEN = 32
CMP_STRIDE = 16
CMP_CHUNKS = CMP_LEN // CMP_STRIDE
CMP_HIDDEN = 128
SEL_LEN = 64
SEL_RATIO = SEL_LEN // CMP_STRIDE
SEL_TOPK = 16
SEL_FORCE = 1e4
WINDOW = 512
NSA_Q_BLOCK = 64
NSA_Q_DIM = NSA_HEADS * NSA_HEAD_DIM
NSA_KV_DIM = NSA_KV_GROUPS * NSA_HEAD_DIM
NSA_IN_DIM = NSA_Q_DIM + 6 * NSA_KV_DIM + 3 * NSA_HEADS

MLA_HEADS = 8
MLA_NOPE_DIM = 128
MLA_ROPE_DIM = 64
MLA_V_DIM = 128
MLA_Q_LORA = 256
MLA_KV_LORA = 256
MLA_IN_DIM = MLA_Q_LORA + MLA_KV_LORA + MLA_ROPE_DIM
ATTN_Q_BLOCK = 128

MOE_GROUPS = 8
MOE_EXPERTS_PER_GROUP = 8
MOE_EXPERTS = MOE_GROUPS * MOE_EXPERTS_PER_GROUP
MOE_TOP_K = 2
MOE_FF = 256
MOE_BLOCK = 128

kernel_name = 'hybrid_nsa_mla_hier_moe'

def rmsnorm(x, g):
    x32 = x.astype(jnp.float32)
    y = x32 * lax.rsqrt(jnp.mean(x32 * x32, axis=-1, keepdims=True) + RMS_EPS)
    return (y * g.astype(jnp.float32)).astype(x.dtype)

def rope_tables(seq, dim):
    inv = 1.0 / (ROPE_THETA ** (jnp.arange(0, dim, 2, dtype=jnp.float32) / dim))
    ang = jnp.arange(seq, dtype=jnp.float32)[:, None] * inv[None, :]
    return jnp.cos(ang), jnp.sin(ang)

def apply_rope(x, cos, sin):
    half = x.shape[-1] // 2
    x32 = x.astype(jnp.float32)
    x1, x2 = x32[..., :half], x32[..., half:]
    c, s = cos[:, None, :], sin[:, None, :]
    return jnp.concatenate([x1 * c - x2 * s, x2 * c + x1 * s], axis=-1).astype(x.dtype)

def masked_softmax(s, mask):
    s = jnp.where(mask, s.astype(jnp.float32), NEG_INF)
    m = jnp.max(s, axis=-1, keepdims=True)
    e = jnp.where(mask, jnp.exp(s - m), 0.0)
    return e / jnp.maximum(jnp.sum(e, axis=-1, keepdims=True), 1e-30)

def sel_overlap_weights():
    offs = np.arange(-(CMP_CHUNKS - 1), SEL_RATIO)
    lo = np.maximum(offs * CMP_STRIDE, 0)
    hi = np.minimum(offs * CMP_STRIDE + CMP_LEN - 1, SEL_LEN - 1)
    return offs, ((hi - lo + 1) / CMP_STRIDE).astype(np.float32)

def nsa_mixer(h, w_in, cmp_pos, cmp_w1, cmp_w2, q_norm, k_norm, w_out, cos, sin):
    B, S, _ = h.shape
    H, G, R, Dh, QB = NSA_HEADS, NSA_KV_GROUPS, NSA_HEADS_PER_GROUP, NSA_HEAD_DIM, NSA_Q_BLOCK
    scale = Dh ** -0.5
    splits = [int(v) for v in np.cumsum([NSA_Q_DIM] + [NSA_KV_DIM] * 6)]
    q, k_c, v_c, k_s, v_s, k_w, v_w, gate_logits = jnp.split(h @ w_in, splits, axis=-1)
    kv = lambda t: t.reshape(B, S, G, Dh)
    q = rmsnorm(q.reshape(B, S, H, Dh), q_norm)
    q_rot = apply_rope(q, cos, sin)

    n_chunks = S // CMP_STRIDE
    n_cmp = n_chunks - CMP_CHUNKS + 1

    def compress(t, pos, w1, w2):
        chunks = t.reshape(B, n_chunks, CMP_STRIDE, G, Dh)
        blocks = jnp.concatenate([chunks[:, i:i + n_cmp] for i in range(CMP_CHUNKS)], axis=2)
        blocks = blocks + pos[None, None, :, None, :]
        flat = blocks.transpose(0, 1, 3, 2, 4).reshape(B, n_cmp, G, CMP_LEN * Dh)
        return jax.nn.gelu(flat @ w1) @ w2

    k_cmp = rmsnorm(compress(kv(k_c), cmp_pos[0], cmp_w1[0], cmp_w2[0]), k_norm[0])
    v_cmp = compress(kv(v_c), cmp_pos[1], cmp_w1[1], cmp_w2[1])
    cmp_end = jnp.arange(n_cmp) * CMP_STRIDE + CMP_LEN - 1

    n_sel = S // SEL_LEN
    sel_k = min(SEL_TOPK, n_sel)
    to_blocks = lambda t: t.reshape(B, n_sel, SEL_LEN, G, Dh).transpose(0, 3, 1, 2, 4)
    k_sel_b = to_blocks(apply_rope(rmsnorm(kv(k_s), k_norm[1]), cos, sin))
    v_sel_b = to_blocks(kv(v_s))
    offs, ow = sel_overlap_weights()
    imp_idx = jnp.asarray(SEL_RATIO * np.arange(n_sel)[:, None] + offs[None, :] + (CMP_CHUNKS - 1))
    imp_w = jnp.asarray(ow)
    back_pad = SEL_RATIO * n_sel - n_cmp
    sel_j = jnp.arange(n_sel)
    b_idx = jnp.arange(B)[:, None, None, None]
    g_idx = jnp.arange(G)[None, :, None, None]

    k_win = apply_rope(rmsnorm(kv(k_w), k_norm[2]), cos, sin)
    pad = ((0, 0), (WINDOW, 0), (0, 0), (0, 0))
    k_win_p, v_win_p = jnp.pad(k_win, pad), jnp.pad(kv(v_w), pad)

    gates = jax.nn.sigmoid(gate_logits.astype(jnp.float32)).reshape(B, S, 3, H).astype(h.dtype)
    nqb = S // QB
    qsplit = lambda t: t.reshape((B, nqb, QB) + t.shape[2:]).swapaxes(0, 1)

    def block(args):
        q_b, qr_b, g_b, bi = args
        t = bi * QB + jnp.arange(QB)
        q_g = q_b.reshape(B, QB, G, R, Dh)
        qr_g = qr_b.reshape(B, QB, G, R, Dh)
        s_c = jnp.einsum('bqgrd,bngd->bgrqn', q_g, k_cmp) * scale
        p_c = masked_softmax(s_c, cmp_end[None, :] <= t[:, None])
        o_c = jnp.einsum('bgrqn,bngd->bqgrd', p_c.astype(v_cmp.dtype), v_cmp)
        imp = jnp.pad(p_c.sum(axis=2), ((0, 0), (0, 0), (0, 0), (CMP_CHUNKS - 1, back_pad)))
        imp = imp[..., imp_idx] @ imp_w
        cur = t // SEL_LEN
        valid = sel_j[None, :] * SEL_LEN <= t[:, None]
        forced = (sel_j[None, :] == 0) | (sel_j[None, :] == cur[:, None]) | (sel_j[None, :] == cur[:, None] - 1)
        score = jnp.where(forced, SEL_FORCE, jnp.where(valid, imp, -1.0))
        _, sel = lax.top_k(score, sel_k)
        k_g = k_sel_b[b_idx, g_idx, sel]
        v_g = v_sel_b[b_idx, g_idx, sel].reshape(B, G, QB, sel_k * SEL_LEN, Dh)
        k_pos = sel[..., None] * SEL_LEN + jnp.arange(SEL_LEN)
        s_s = jnp.einsum('bqgrd,bgqkld->bgrqkl', qr_g, k_g) * scale
        s_mask = (k_pos <= t[None, None, :, None, None]).reshape(B, G, 1, QB, sel_k * SEL_LEN)
        p_s = masked_softmax(s_s.reshape(B, G, R, QB, sel_k * SEL_LEN), s_mask)
        o_s = jnp.einsum('bgrqk,bgqkd->bqgrd', p_s.astype(v_g.dtype), v_g)
        k_wb = lax.dynamic_slice_in_dim(k_win_p, bi * QB, QB + WINDOW, axis=1)
        v_wb = lax.dynamic_slice_in_dim(v_win_p, bi * QB, QB + WINDOW, axis=1)
        kp = bi * QB - WINDOW + jnp.arange(QB + WINDOW)
        w_mask = (kp[None, :] <= t[:, None]) & (kp[None, :] > t[:, None] - WINDOW) & (kp[None, :] >= 0)
        s_w = jnp.einsum('bqgrd,bkgd->bgrqk', qr_g, k_wb) * scale
        p_w = masked_softmax(s_w, w_mask)
        o_w = jnp.einsum('bgrqk,bkgd->bqgrd', p_w.astype(v_wb.dtype), v_wb)
        return (g_b[:, :, 0, :, None] * o_c.reshape(B, QB, H, Dh)
                + g_b[:, :, 1, :, None] * o_s.reshape(B, QB, H, Dh)
                + g_b[:, :, 2, :, None] * o_w.reshape(B, QB, H, Dh))

    o = lax.map(block, (qsplit(q), qsplit(q_rot), qsplit(gates), jnp.arange(nqb)))
    return o.swapaxes(0, 1).reshape(B, S, NSA_Q_DIM) @ w_out

def mla_mixer(h, w_in, q_lat_norm, kv_lat_norm, w_uq, w_ukv, q_nope_norm, q_rope_norm,
              k_nope_norm, k_rope_norm, w_out, cos, sin):
    B, S, _ = h.shape
    H = MLA_HEADS
    c_q, c_kv, k_r = jnp.split(h @ w_in, [MLA_Q_LORA, MLA_Q_LORA + MLA_KV_LORA], axis=-1)
    q = (rmsnorm(c_q, q_lat_norm) @ w_uq).reshape(B, S, H, MLA_NOPE_DIM + MLA_ROPE_DIM)
    kvu = (rmsnorm(c_kv, kv_lat_norm) @ w_ukv).reshape(B, S, H, MLA_NOPE_DIM + MLA_V_DIM)
    q_nope = rmsnorm(q[..., :MLA_NOPE_DIM], q_nope_norm)
    q_rope = apply_rope(rmsnorm(q[..., MLA_NOPE_DIM:], q_rope_norm), cos, sin)
    k_nope = rmsnorm(kvu[..., :MLA_NOPE_DIM], k_nope_norm)
    v = kvu[..., MLA_NOPE_DIM:]
    k_rope = apply_rope(rmsnorm(k_r.reshape(B, S, 1, MLA_ROPE_DIM), k_rope_norm), cos, sin)[:, :, 0]
    scale = (MLA_NOPE_DIM + MLA_ROPE_DIM) ** -0.5
    outs = []
    for start in range(0, S, ATTN_Q_BLOCK):
        end = start + ATTN_Q_BLOCK
        s = (jnp.einsum('bqhd,bkhd->bhqk', q_nope[:, start:end], k_nope[:, :end])
             + jnp.einsum('bqhd,bkd->bhqk', q_rope[:, start:end], k_rope[:, :end])) * scale
        mask = jnp.arange(end)[None, :] <= jnp.arange(start, end)[:, None]
        p = masked_softmax(s, mask)
        outs.append(jnp.einsum('bhqk,bkhd->bqhd', p.astype(v.dtype), v[:, :end]))
    o = jnp.concatenate(outs, axis=1).reshape(B, S, H * MLA_V_DIM)
    return o @ w_out

def hier_moe(x2, w_group, b_group, w_expert, b_expert, w_gate, w_up, w_down):
    T, D = x2.shape
    g_prob = jax.nn.softmax((x2 @ w_group + b_group).astype(jnp.float32), axis=-1)
    grp = jnp.argmax(g_prob, axis=-1)
    g_w = jnp.take_along_axis(g_prob, grp[:, None], axis=-1)
    e_logits = (x2 @ w_expert + b_expert).astype(jnp.float32).reshape(T, MOE_GROUPS, MOE_EXPERTS_PER_GROUP)
    e_logits = jnp.take_along_axis(e_logits, grp[:, None, None], axis=1)[:, 0]
    top_p, top_i = lax.top_k(jax.nn.softmax(e_logits, axis=-1), MOE_TOP_K)
    weights = (g_w * top_p / jnp.sum(top_p, axis=-1, keepdims=True)).astype(x2.dtype)
    expert_id = grp[:, None] * MOE_EXPERTS_PER_GROUP + top_i
    n_assign = T * MOE_TOP_K
    flat_e = expert_id.reshape(n_assign)
    flat_tok = jnp.arange(n_assign, dtype=jnp.int32) // MOE_TOP_K
    order = jnp.argsort(flat_e)
    sorted_e = flat_e[order]
    counts = jnp.bincount(flat_e, length=MOE_EXPERTS)
    starts = jnp.cumsum(counts) - counts
    padded = (counts + MOE_BLOCK - 1) // MOE_BLOCK * MOE_BLOCK
    pad_ends = jnp.cumsum(padded)
    pad_starts = pad_ends - padded
    dest = pad_starts[sorted_e] + jnp.arange(n_assign) - starts[sorted_e]
    n_blocks = -(-n_assign // MOE_BLOCK) + MOE_EXPERTS
    n_slots = n_blocks * MOE_BLOCK
    slot_tok = jnp.full((n_slots,), T, jnp.int32).at[dest].set(flat_tok[order])
    slot_w = jnp.zeros((n_slots,), x2.dtype).at[dest].set(weights.reshape(n_assign)[order])
    block_e = jnp.minimum(jnp.searchsorted(pad_ends, jnp.arange(n_blocks) * MOE_BLOCK, side='right'),
                          MOE_EXPERTS - 1)
    x_pad = jnp.concatenate([x2, jnp.zeros((1, D), x2.dtype)], axis=0)
    xs = x_pad[slot_tok].reshape(n_blocks, MOE_BLOCK, D)

    def expert_block(args):
        xb, e = args
        return (jax.nn.silu(xb @ w_gate[e]) * (xb @ w_up[e])) @ w_down[e]

    ys = lax.map(expert_block, (xs, block_e)).reshape(n_slots, D) * slot_w[:, None]
    return jnp.zeros((T + 1, D), ys.dtype).at[slot_tok].add(ys)[:T]

def setup_inputs(seed: int = 0) -> dict:
    key = jax.random.key(seed)
    ks = iter(jax.random.split(key, 32))

    def nrm(shape, scale):
        return jax.random.normal(next(ks), shape, jnp.float32) * scale

    def gain(shape):
        return 1.0 + 0.1 * nrm(shape, 1.0)

    LA, LB, L = N_NSA_LAYERS, N_MLA_LAYERS, DEPTH
    return {
        'x': nrm((BATCH, SEQ, D_MODEL), 1.0),
        'norm_mix': gain((L, D_MODEL)),
        'norm_ffn': gain((L, D_MODEL)),
        'nsa_w_in': nrm((LA, D_MODEL, NSA_IN_DIM), D_MODEL ** -0.5),
        'nsa_cmp_pos': nrm((LA, 2, CMP_LEN, NSA_HEAD_DIM), 0.1),
        'nsa_cmp_w1': nrm((LA, 2, CMP_LEN * NSA_HEAD_DIM, CMP_HIDDEN), (CMP_LEN * NSA_HEAD_DIM) ** -0.5),
        'nsa_cmp_w2': nrm((LA, 2, CMP_HIDDEN, NSA_HEAD_DIM), CMP_HIDDEN ** -0.5),
        'nsa_q_norm': gain((LA, NSA_HEAD_DIM)),
        'nsa_k_norm': gain((LA, 3, NSA_HEAD_DIM)),
        'nsa_w_out': nrm((LA, NSA_Q_DIM, D_MODEL), NSA_Q_DIM ** -0.5),
        'mla_w_in': nrm((LB, D_MODEL, MLA_IN_DIM), D_MODEL ** -0.5),
        'mla_q_lat_norm': gain((LB, MLA_Q_LORA)),
        'mla_kv_lat_norm': gain((LB, MLA_KV_LORA)),
        'mla_w_uq': nrm((LB, MLA_Q_LORA, MLA_HEADS * (MLA_NOPE_DIM + MLA_ROPE_DIM)), MLA_Q_LORA ** -0.5),
        'mla_w_ukv': nrm((LB, MLA_KV_LORA, MLA_HEADS * (MLA_NOPE_DIM + MLA_V_DIM)), MLA_KV_LORA ** -0.5),
        'mla_q_nope_norm': gain((LB, MLA_NOPE_DIM)),
        'mla_q_rope_norm': gain((LB, MLA_ROPE_DIM)),
        'mla_k_nope_norm': gain((LB, MLA_NOPE_DIM)),
        'mla_k_rope_norm': gain((LB, MLA_ROPE_DIM)),
        'mla_w_out': nrm((LB, MLA_HEADS * MLA_V_DIM, D_MODEL), (MLA_HEADS * MLA_V_DIM) ** -0.5),
        'moe_w_group': nrm((L, D_MODEL, MOE_GROUPS), D_MODEL ** -0.5),
        'moe_b_group': nrm((L, MOE_GROUPS), 0.01),
        'moe_w_expert': nrm((L, D_MODEL, MOE_EXPERTS), D_MODEL ** -0.5),
        'moe_b_expert': nrm((L, MOE_EXPERTS), 0.01),
        'moe_w_gate': nrm((L, MOE_EXPERTS, D_MODEL, MOE_FF), D_MODEL ** -0.5),
        'moe_w_up': nrm((L, MOE_EXPERTS, D_MODEL, MOE_FF), D_MODEL ** -0.5),
        'moe_w_down': nrm((L, MOE_EXPERTS, MOE_FF, D_MODEL), MOE_FF ** -0.5),
    }

def reference(x, norm_mix, norm_ffn, nsa_w_in, nsa_cmp_pos, nsa_cmp_w1, nsa_cmp_w2, nsa_q_norm,
              nsa_k_norm, nsa_w_out, mla_w_in, mla_q_lat_norm, mla_kv_lat_norm, mla_w_uq, mla_w_ukv,
              mla_q_nope_norm, mla_q_rope_norm, mla_k_nope_norm, mla_k_rope_norm, mla_w_out,
              moe_w_group, moe_b_group, moe_w_expert, moe_b_expert, moe_w_gate, moe_w_up, moe_w_down):
    B, S, D = x.shape
    cos_a, sin_a = rope_tables(S, NSA_HEAD_DIM)
    cos_b, sin_b = rope_tables(S, MLA_ROPE_DIM)
    for i in range(DEPTH):
        j = i // N_MIXERS
        h = rmsnorm(x, norm_mix[i])
        if i % N_MIXERS == 0:
            mix = nsa_mixer(h, nsa_w_in[j], nsa_cmp_pos[j], nsa_cmp_w1[j], nsa_cmp_w2[j],
                            nsa_q_norm[j], nsa_k_norm[j], nsa_w_out[j], cos_a, sin_a)
        else:
            mix = mla_mixer(h, mla_w_in[j], mla_q_lat_norm[j], mla_kv_lat_norm[j], mla_w_uq[j],
                            mla_w_ukv[j], mla_q_nope_norm[j], mla_q_rope_norm[j], mla_k_nope_norm[j],
                            mla_k_rope_norm[j], mla_w_out[j], cos_b, sin_b)
        x = x + mix
        h = rmsnorm(x, norm_ffn[i]).reshape(B * S, D)
        x = x + hier_moe(h, moe_w_group[i], moe_b_group[i], moe_w_expert[i], moe_b_expert[i],
                         moe_w_gate[i], moe_w_up[i], moe_w_down[i]).reshape(B, S, D)
    return x


_drawn_inputs = setup_inputs


def setup_inputs(seed=0):
    import zlib

    import numpy as np

    out = dict(_drawn_inputs(seed))
    spreads = {}
    factors = {'mla_q_lat_norm': 2.793,
     'mla_q_nope_norm': 2.785,
     'mla_q_rope_norm': 3.368,
     'mla_k_rope_norm': 3.432,
     'moe_b_group': 3.104,
     'moe_b_expert': 2.982}
    for name, (base, spread) in spreads.items():
        noise = np.random.default_rng([zlib.crc32(name.encode()), seed]).standard_normal(out[name].shape)
        drawn = base * np.exp(spread * noise) if base else spread * noise
        out[name] = jnp.asarray(drawn.astype(out[name].dtype))
    for name, factor in factors.items():
        out[name] = (out[name] * factor).astype(out[name].dtype)
    return out
```

```python
from contextlib import ExitStack

import numpy as np

import concourse.bass as bass
from concourse import mybir

F32 = mybir.dt.float32
I32 = mybir.dt.int32
U32 = mybir.dt.uint32
ALU = mybir.AluOpType
ACT = mybir.ActivationFunctionType
AX = mybir.AxisListType.X

P = 128
D = 1024
S = 512
TILES = S // P
KD = D // P
LAYERS = 2
EPS = 1e-6
NEG = -1e30

GROUPS = 8
PER_GROUP = 8
EXPERTS = GROUPS * PER_GROUP
ROUTER = GROUPS + EXPERTS
TOPK = 2
FF = 256
ROWS = S * TOPK
CHUNKS = ROWS // P
BLOCK = 64
SLOTS = 4
IN_BUFFERS = 3
MAX_EXTRA = ROWS // BLOCK

KV_GROUPS = 4
SHARE = 4
NSA_HEADS = KV_GROUPS * SHARE
DH = 64
CMP_LEN = 32
CMP_STRIDE = 16
N_CMP = S // CMP_STRIDE - 1
CMP_SLOTS = 32
CMP_HIDDEN = 128
GROUP_IN = (SHARE + 6) * DH
Q_COLS = SHARE * DH
NORMED = Q_COLS + 2 * DH
GATES = 3 * NSA_HEADS
UNITS = 2 * SHARE

HEADS = 8
NOPE = 128
ROPE = 64
QK = NOPE + ROPE
VDIM = 128
LORA = 256
MLA_IN = 2 * LORA + ROPE
HEAD_COLS = QK + NOPE + VDIM
MLA_SCALE = QK ** -0.5


class Chain:

    def __init__(self, engine, semaphore):
        self.engine, self.semaphore, self.count, self.turn = engine, semaphore, 0, None

    def value(self):
        if self.turn is None:
            return self.count
        return self.turn * self.each + self.count

    def __call__(self, instruction):
        self.mark(instruction)
        self.join()

    def enter(self, turn, each):
        self.turn, self.each, self.before = turn, each, self.count

    def leave(self, turns):
        assert self.count - self.before == self.each, (self.count - self.before, self.each)
        self.turn = None
        self.count = self.before + turns * self.each

    def mark(self, instruction):
        self.count = self.count + 1
        instruction.then_inc(self.semaphore, 1)

    def join(self):
        self.engine.wait_ge(self.semaphore, self.value())


def build(nc, a, out, stages):
    with ExitStack() as ctx:
        def sb(name, shape, dt=F32):
            return ctx.enter_context(nc.sbuf_tensor("sb_" + name, shape, dt))

        def sem(name):
            return ctx.enter_context(nc.semaphore(name))

        ps = ctx.enter_context(nc.psum_tensor("ps", [P, 8, 512], F32))

        x = sb("x_res", [P, TILES, D])
        h = sb("h_norm", [P, TILES, D])
        hT = sb("hT", [P, KD, S])
        gain = sb("gain", [P, D])
        ssq = sb("ssq", [P, TILES])
        rstd = sb("rstd", [P, TILES])
        ident = sb("ident", [P, P])
        minus_half = sb("minus_half", [P, 1])
        ring = sb("ring", [P, SLOTS, 3, KD * FF])
        xsT = sb("xsT", [P, KD, ROWS + BLOCK])
        x_block = sb("x_block", [P, 2, KD, BLOCK])
        silu = sb("silu", [P, P])
        hid = sb("hid", [P, P])
        hidT = sb("hidT", [P, P])
        y_sb = sb("y_sb", [P, 2, 512])
        w_router = sb("w_router", [P, KD, ROUTER])
        b_router = sb("b_router", [P, ROUTER])
        ones = sb("ones", [P, P])
        below = sb("below", [P, P])
        falling = sb("falling", [P, 8])
        expert_no = sb("expert_no", [P, EXPERTS])
        part_no = sb("part_no", [P, 1])
        y_flat = y_sb[:, :, :].rearrange("p b n -> p (b n)")
        logit = y_flat[:, 0:TILES * ROUTER].rearrange("p (t n) -> p t n", t=TILES)
        r8 = y_flat[:, 288:544].rearrange("p (i t n) -> p i t n", i=8, t=TILES)
        placed = y_flat[:, 544:800].rearrange("p (t e) -> p t e", t=TILES)
        r1 = sb("r1", [P, 8, TILES])
        pos = sb("pos", [P, TOPK, TILES])
        pos_u = sb("pos_u", [P, TOPK * TILES], U32)
        wt = sb("wt", [P, TOPK, TILES])
        count = sb("count", [P, 6, EXPERTS])
        start_i = sb("start_i", [1, LAYERS, EXPERTS + 1], I32)
        count_i = sb("count_i", [1, LAYERS, EXPERTS], I32)
        extra_f = sb("extra_f", [P, 8])
        extra_i = sb("extra_i", [P, 2], I32)
        extra_n = sb("extra_n", [1, LAYERS], I32)
        extra_t = sb("extra_t", [1, LAYERS, 2, MAX_EXTRA], I32)
        xs_in = hT[:, 0:2 * IN_BUFFERS, :].rearrange("p (b j) n -> p b (j n)", b=IN_BUFFERS)
        pick = hT[:, 6:8, :].rearrange("p k n -> p (k n)")[:, 0:3 * TILES * EXPERTS].rearrange(
            "p (i t e) -> p i t e", i=3, t=TILES)
        place = hT[:, 7, S - TILES * EXPERTS:S].rearrange("p (t e) -> p t e", t=TILES)
        y_in = xsT[:, :, :].rearrange("p k n -> p (k n)")[:, 0:TOPK * TILES * D].rearrange(
            "p (b n) -> p b n", b=TOPK * TILES)

        xs_dram = nc.dram_tensor("sorted_rows", (ROWS, D), F32, kind="Internal").ap()
        ys_dram = nc.dram_tensor("expert_rows", (ROWS + BLOCK, D), F32, kind="Internal").ap()

        work = ring[:, 1:SLOTS].rearrange("p s i n -> p (s i n)")
        scratch = xsT[:, :, :].rearrange("p k n -> p (k n)")
        h_space = h[:, :, :].rearrange("p t n -> p (t n)")
        hT_space = hT[:, :, :].rearrange("p k n -> p (k n)")
        o_rows = scratch[:, 0:TILES * D].rearrange("p (t n) -> p t n", t=TILES)
        probs = x_block[:, :, :, :].rearrange("p b k n -> p b (k n)")
        probsT = y_sb
        row_max = sb("row_max", [P, TILES])
        row_sum = sb("row_sum", [P, TILES])
        row_inv = sb("row_inv", [P, TILES])
        tri = sb("tri", [P, P])
        turn = sb("turn", [P, 2, TILES, ROPE])

        def cut(space, at, *shape):
            size = int(np.prod(shape))
            v = space[:, at:at + size]
            if len(shape) == 2:
                v = v.rearrange("p (a b) -> p a b", a=shape[0])
            if len(shape) == 3:
                v = v.rearrange("p (a b c) -> p a b c", a=shape[0], b=shape[1])
            return v, at + size

        mla_gain = sb("mla_gain", [P, 2 * LORA + 2 * QK])
        mean_sq = sb("mean_sq", [P, 3, TILES])
        w_uq, at = cut(work, 0, 2, HEADS * QK)
        w_ukv, at = cut(work, at, 2, HEADS * (NOPE + VDIM))
        w_out, end = cut(work, at, KD, D)
        w_in, _ = cut(work, at, KD, MLA_IN)
        head, at = cut(work, end, TILES, HEAD_COLS)
        q_rows, at = cut(work, at, TILES, QK)
        k_rows, at = cut(work, at, TILES, NOPE)
        squares, at = cut(scratch, TILES * D, TILES, QK + NOPE)
        rope_a, at = cut(scratch, at, TILES, ROPE)
        rope_b, at = cut(scratch, at, TILES, ROPE)
        c_rows, at = cut(h_space, 0, 2, MLA_IN)
        cT, at = cut(h_space, at, 4, S)
        kr_rows, at = cut(h_space, at, TILES, ROPE)
        qnT, at = cut(hT_space, 0, S)
        knT, at = cut(hT_space, at, S)
        qrT, at = cut(hT_space, at, S)
        krT, at = cut(hT_space, at, S)

        nsa_w_out, _ = cut(work, 0, KD, D)
        w_group, at = cut(work, 0, KD, GROUP_IN)
        w_gates, at = cut(work, at, KD, GATES)
        own, at = cut(work, KD * D, TILES, GROUP_IN)
        qk_rot, at = cut(work, at, TILES, NORMED)
        spare, at = cut(work, at, 4 * S)
        ks_low, at = cut(work, at, S)
        ks_high, at = cut(work, at, S)
        kw_low, at = cut(work, at, S)
        kw_high, at = cut(work, at, S)
        rot_tmp = spare[:, 0:TILES * NORMED].rearrange("p (t n) -> p t n", t=TILES)
        kcvT = spare[:, 0:S]
        cmpT = spare[:, S:2 * S]
        cmp_out = spare[:, 2 * S:4 * S].rearrange("p (t r d) -> p t r d", t=TILES, r=SHARE)
        q_pair, at = cut(scratch, TILES * D, 2, S)
        qr_pair, at = cut(scratch, at, 2, S)
        v_blocks, at = cut(scratch, at, SHARE, DH)
        k_blocks, at = cut(scratch, at, 2 * CMP_SLOTS)
        cmp_probs, at = cut(scratch, at, TILES * SHARE, CMP_SLOTS)
        cmp_p4 = cmp_probs.rearrange("p (t r) n -> p t r n", t=TILES)
        hidden, at = cut(scratch, at, 2, CMP_SLOTS)
        k_cmp, at = cut(scratch, at, 2, DH)
        cmp_w1 = h_space.rearrange("p (l n) -> p l n", l=CMP_LEN)
        cmp_bias = sb("cmp_bias", [P, 2])
        at = KD * D + TILES * (GROUP_IN + NORMED) + 8 * S
        cmp_w2, at = cut(work, at, 2, DH)
        cmp_pos, at = cut(work, at, CMP_LEN)
        cmp_mask, at = cut(work, at, 2, TILES, CMP_SLOTS)
        nsa_gain, at = cut(work, at, SHARE + 3, DH)
        gates, at = cut(work, at, TILES, GATES)
        group_ms = sb("group_ms", [P, TILES, SHARE + 2])
        weight = sb("weight", [P, TILES])
        kc_ms = sb("kc_ms", [P, 1])
        c_max = sb("c_max", [P, TILES * SHARE])
        c_sum = sb("c_sum", [P, TILES * SHARE])

        group_loaded = sem("group_loaded")
        gates_loaded = sem("gates_loaded")
        cmp_loaded = sem("cmp_loaded")
        gates_done = sem("gates_done")
        gates_exp = sem("gates_exp")
        gates_taken = sem("gates_taken")
        bias_done = sem("bias_done")
        bias_ready = sem("bias_ready")
        group_done = sem("group_done")
        group_taken = sem("group_taken")
        g_squared = sem("g_squared")
        g_summed = sem("g_summed")
        g_scales = sem("g_scales")
        g_staged = sem("g_staged")
        g_turned = sem("g_turned")
        gT_act = sem("gT_act")
        gT_dve = sem("gT_dve")
        packed = sem("packed")
        gelu_done = sem("gelu_done")
        cmp_made = sem("cmp_made")
        kc_summed = sem("kc_summed")
        kc_scale = sem("kc_scale")
        kc_staged = sem("kc_staged")
        kc_turned = sem("kc_turned")
        kc_ready = sem("kc_ready")
        vc_ready = sem("vc_ready")
        c_scored = sem("c_scored")
        c_shifted = sem("c_shifted")
        c_exp = sem("c_exp")
        c_probs = sem("c_probs")
        c_probsT = sem("c_probsT")
        c_probsT_ready = sem("c_probsT_ready")
        c_weighed = sem("c_weighed")
        small_loaded = sem("small_loaded")
        mla_gain_ready = sem("mla_gain_ready")
        mla_in_loaded = sem("mla_in_loaded")
        mla_up_loaded = sem("mla_up_loaded")
        out_loaded = sem("out_loaded")
        c_done = sem("c_done")
        c_squares = sem("c_squares")
        c_scales = sem("c_scales")
        c_ready = sem("c_ready")
        c_turned = sem("c_turned")
        cT_ready = sem("cT_ready")
        kr_staged = sem("kr_staged")
        kr_turned = sem("kr_turned")
        krT_ready = sem("krT_ready")
        head_done = sem("head_done")
        head_taken = sem("head_taken")
        sq_done = sem("sq_done")
        ms_ready = sem("ms_ready")
        rs_ready = sem("rs_ready")
        qk_staged = sem("qk_staged")
        qk_turned = sem("qk_turned")
        qkT_act = sem("qkT_act")
        qkT_dve = sem("qkT_dve")
        scores_done = sem("scores_done")
        max_done = sem("max_done")
        exp_done = sem("exp_done")
        probs_turned = sem("probs_turned")
        probsT_ready = sem("probsT_ready")
        pv_done = sem("pv_done")
        o_taken = sem("o_taken")
        out_done = sem("out_done")
        out_added = sem("out_added")
        gain_used = sem("gain_used")
        x_loaded = sem("x_loaded")
        gain_loaded = sem("gain_loaded")
        consts_ready = sem("consts_ready")
        pool_step = sem("pool_step")
        x_ready = sem("x_ready")
        ssq_ready = sem("ssq_ready")
        rstd_ready = sem("rstd_ready")
        h_ready = sem("h_ready")
        h_turned = sem("h_turned")
        hT_act = sem("hT_act")
        hT_dve = sem("hT_dve")
        dve_step = sem("dve_step")
        router_loaded = sem("router_loaded")
        logits_done = sem("logits_done")
        group_shift = sem("group_shift")
        group_exp = sem("group_exp")
        pair_shift = sem("pair_shift")
        pair_exp = sem("pair_exp")
        picks_ready = sem("picks_ready")
        counted = sem("counted")
        pos_ready = sem("pos_ready")
        tables_ready = sem("tables_ready")
        scattered = sem("scattered")
        chunk_loaded = [sem(f"chunk_loaded{i}") for i in range(CHUNKS)]
        chunk_turned = sem("chunk_turned")
        xsT_act = sem("xsT_act")
        xsT_dve = sem("xsT_dve")
        up_loaded = [sem(f"up_loaded{i}") for i in range(SLOTS)]
        down_loaded = [sem(f"down_loaded{i}") for i in range(SLOTS)]
        block_ready = sem("block_ready")
        up_done = sem("up_done")
        silu_done = sem("silu_done")
        hid_done = sem("hid_done")
        hid_turned = sem("hid_turned")
        hidT_ready = sem("hidT_ready")
        down_done = sem("down_done")
        y_ready = sem("y_ready")
        y_written = sem("y_written")
        y_free = sem("y_free")
        extra_sent = sem("extra_sent")
        extra_made = sem("extra_made")
        ex = [{n: sem(f"extra{l}_{n}") for n in
               ("loaded", "block", "up", "silu", "hid", "turned", "hidT", "down", "y", "written", "over")}
              for l in range(LAYERS)]
        gathered = [sem(f"gathered{i}") for i in range(TOPK * TILES)]
        stored = sem("stored")

        PHASES = 2 * LAYERS
        OUT_PARTS = 2 * TILES
        Y_FIRST = 16
        NSA_UNITS = 32 if 0 in stages else 0
        MLA_STEPS = 16
        NSA_STEPS = 18 + 6 * UNITS
        SMALL = 16 * (17 if 0 in stages else 7)

        def expert_weights(eng, l, e, slot):
            gate = a["moe_w_gate"][l, e] if isinstance(e, int) else a["moe_w_gate"][l, bass.ds(e, 1)].rearrange("e k f -> (e k) f")
            up = a["moe_w_up"][l, e] if isinstance(e, int) else a["moe_w_up"][l, bass.ds(e, 1)].rearrange("e k f -> (e k) f")
            down = a["moe_w_down"][l, e] if isinstance(e, int) else a["moe_w_down"][l, bass.ds(e, 1)].rearrange("e k f -> (e k) f")
            return (
                eng.dma_start(ring[:, slot, 0, :], gate.rearrange("(p k) f -> p (k f)", k=KD)),
                eng.dma_start(ring[:, slot, 1, :], up.rearrange("(p k) f -> p (k f)", k=KD)),
                eng.dma_start(ring[:, slot, 2, :].rearrange("p (c n) -> p c n", c=FF // P),
                              down.rearrange("(c p) n -> p c n", p=P)),
            )

        block = ctx.enter_context(nc.Block())

        @block.sync
        def _(sp):
            for t in range(TILES):
                sp.dma_start(x[:, t, :], a["x"][t * P:(t + 1) * P, :]).then_inc(x_loaded, 16)

            def moe_loads(l):
                done = l * EXPERTS
                for u in range(SLOTS):
                    if l > 0 and u == 0:
                        sp.wait_ge(down_done, done)
                    if u == 1 and 2 * l in stages:
                        sp.wait_ge(out_done, OUT_PARTS * (mixers[0]))
                    g, up, dn = expert_weights(sp, l, u, u)
                    g.then_inc(up_loaded[u], 16)
                    up.then_inc(up_loaded[u], 16)
                    dn.then_inc(down_loaded[u], 16)
                sp.wait_ge(scattered, 16 * TOPK * TILES * (l + 1))
                for c in range(CHUNKS):
                    if c >= IN_BUFFERS:
                        sp.wait_ge(chunk_turned, l * CHUNKS + c - IN_BUFFERS + 1)
                    sp.dma_start(xs_in[:, c % IN_BUFFERS, :], xs_dram[c * P:(c + 1) * P, :]).then_inc(chunk_loaded[c], 16)
                with sp.Fori(1, EXPERTS // SLOTS) as i:
                    for u in range(SLOTS):
                        sp.wait_ge(down_done, (i - 1) * SLOTS + (done + u + 1))
                        g, up, dn = expert_weights(sp, l, i * SLOTS + u, u)
                        g.then_inc(up_loaded[u], 16)
                        up.then_inc(up_loaded[u], 16)
                        dn.then_inc(down_loaded[u], 16)
                sp.wait_ge(extra_made, 16 * 2 * (l + 1))
                n = sp.value_load(extra_n[0:1, l:l + 1], min_val=0, max_val=MAX_EXTRA)
                with sp.If(n > 0):
                    sp.wait_ge(down_done, done + EXPERTS)
                    sp.sem_inc(ex[l]["down"], 1)
                    with sp.Fori(0, n) as q:
                        e = sp.value_load(extra_t[0:1, l, 0, bass.ds(q, 1)], min_val=0, max_val=EXPERTS - 1)
                        sp.wait_ge(ex[l]["down"], q + 1)
                        for load in expert_weights(sp, l, e, 0):
                            load.then_inc(ex[l]["loaded"], 16)
                    sp.wait_ge(ex[l]["down"], n + 1)
                    sp.sem_inc(ex[l]["over"], 1)

            mixers = [0]

            def mla_loads():
                sp.wait_ge(down_done, EXPERTS * (1 in stages))
                sp.dma_start(w_in, a["mla_w_in"].rearrange("(p k) n -> p k n", k=KD)).then_inc(mla_in_loaded, 16)
                sp.dma_start(w_uq, a["mla_w_uq"].rearrange("(c p) n -> p c n", p=P)).then_inc(mla_up_loaded, 16)
                sp.dma_start(w_ukv, a["mla_w_ukv"].rearrange("(c p) n -> p c n", p=P)).then_inc(mla_up_loaded, 16)
                sp.wait_ge(c_done, TILES)
                mixers[0] += 1
                sp.dma_start(w_out, a["mla_w_out"].rearrange("(p k) n -> p k n", k=KD)).then_inc(out_loaded, 16)

            def nsa_loads():
                sp.dma_start(w_gates, a["nsa_w_gates"]).then_inc(gates_loaded, 16)
                sp.dma_start(w_group, a["nsa_w_group"][0]).then_inc(group_loaded, 16)
                sp.wait_ge(h_turned, 2 * TILES)
                sp.dma_start(cmp_w1, a["nsa_cmp_w1"]).then_inc(cmp_loaded, 16)
                with sp.Fori(1, KV_GROUPS) as i:
                    sp.wait_ge(group_done, i * TILES)
                    sp.dma_start(w_group, a["nsa_w_group"][bass.ds(i, 1)].rearrange("g p k n -> (g p) k n")).then_inc(group_loaded, 16)
                sp.wait_ge(group_done, KV_GROUPS * TILES)
                mixers[0] += 1
                sp.dma_start(nsa_w_out, a["nsa_w_out"].rearrange("(p k) n -> p k n", k=KD)).then_inc(out_loaded, 16)

            for ph in range(PHASES):
                if ph not in stages:
                    continue
                if ph == 0:
                    nsa_loads()
                if ph == 2:
                    mla_loads()
                if ph % 2 == 1:
                    moe_loads(ph // 2)
            sp.wait_ge(x_ready, TILES * (len(stages)))
            for t in range(TILES):
                sp.dma_start(out[t * P:(t + 1) * P, :], x[:, t, :]).then_inc(stored, 16)
            sp.wait_ge(stored, 16 * TILES)

        @block.gpsimd
        def _(pool):
            step = Chain(pool, pool_step)
            step(pool.memset(ones[:, :], 1.0))
            step(pool.memset(minus_half[:, :], -0.5))
            step(pool.affine_select(out=ident[:, :], in_=ones[:, :], compare_op=ALU.is_equal, fill=0.0,
                                    base=0, pattern=[[-1, P]], channel_multiplier=1))
            step(pool.affine_select(out=below[:, :], in_=ones[:, :], compare_op=ALU.is_gt, fill=0.0,
                                    base=0, pattern=[[1, P]], channel_multiplier=-1))
            step(pool.iota(falling[:, :], pattern=[[-1, 8]], base=8, channel_multiplier=0,
                           allow_small_or_imprecise_dtypes=True))
            step(pool.iota(expert_no[:, :], pattern=[[1, EXPERTS]], base=0, channel_multiplier=0,
                           allow_small_or_imprecise_dtypes=True))
            pool.iota(part_no[:, :], pattern=[[0, 1]], base=0, channel_multiplier=1,
                      allow_small_or_imprecise_dtypes=True).then_inc(consts_ready, 1)

            step(pool.memset(tri[:, :], 0.0))
            pool.affine_select(out=tri[:, :], in_=tri[:, :], compare_op=ALU.is_ge, fill=NEG,
                               base=0, pattern=[[-1, P]], channel_multiplier=1).then_inc(consts_ready, 1)
            pool.dma_start(turn[:, :, :, :], a["rope"]).then_inc(small_loaded, 16)
            at = 0
            for name, size in (("q_lat_norm", LORA), ("kv_lat_norm", LORA), ("q_nope_norm", NOPE),
                               ("q_rope_norm", ROPE), ("k_nope_norm", NOPE), ("k_rope_norm", ROPE)):
                pool.dma_start(mla_gain[:, at:at + size], a["mla_" + name].partition_broadcast(P)).then_inc(small_loaded, 16)
                at += size
            for i, g in enumerate(() if 0 not in stages else ("nsa_q_norm", "nsa_k_norm_1", "nsa_k_norm_2", "nsa_k_norm_0")):
                for r in (range(SHARE) if i == 0 else (SHARE + i - 1,)):
                    pool.dma_start(nsa_gain[:, r, :], a[g].partition_broadcast(P)).then_inc(small_loaded, 16)
            if 0 in stages:
                pool.dma_start(cmp_mask[:, :, :, :], a["cmp_mask"]).then_inc(small_loaded, 16)
                pool.dma_start(cmp_w2[:, :, :], a["nsa_cmp_w2"]).then_inc(small_loaded, 16)
                pool.dma_start(cmp_pos[:, :], a["nsa_cmp_pos"]).then_inc(small_loaded, 16)
            norms = [0]

            def nsa_scales():
                with pool.Fori(0, KV_GROUPS) as i:
                    pool.wait_ge(g_summed, i + 1)
                    pool.tensor_tensor(group_ms[:, :, :], group_ms[:, :, :],
                                       minus_half[:, 0:1].unsqueeze(1).to_broadcast([P, TILES, SHARE + 2]), ALU.pow
                                       ).then_inc(g_scales, 1)
                    pool.wait_ge(kc_summed, i + 1)
                    pool.tensor_tensor(kc_ms[:, :], kc_ms[:, :], minus_half[:, :], ALU.pow
                                       ).then_inc(kc_scale, 1)

            def mla_scales():
                c_ms = mean_sq[:, :, :]
                for t in range(TILES):
                    pool.wait_ge(c_squares, t + 1)
                    step(pool.tensor_scalar(c_ms[:, :, t], c_ms[:, :, t], EPS, None, ALU.add))
                    pool.tensor_tensor(c_ms[:, :, t], c_ms[:, :, t], minus_half[:, 0:1].to_broadcast([P, 3]),
                                       ALU.pow).then_inc(c_scales, 1)
                with pool.Fori(0, HEADS) as i:
                    pool.wait_ge(ms_ready, i + 1)
                    pool.tensor_tensor(mean_sq[:, :, :], mean_sq[:, :, :],
                                       minus_half[:, 0:1].unsqueeze(1).to_broadcast([P, 3, TILES]), ALU.pow
                                       ).then_inc(rs_ready, 1)

            def gains(ph):
                g = a["norm_ffn"] if ph % 2 else a["norm_mix"]
                if norms[0]:
                    pool.wait_ge(gain_used, norms[0])
                norms[0] += 1
                pool.dma_start(gain[:, :], g[ph // 2:ph // 2 + 1, :].partition_broadcast(P)
                               ).then_inc(gain_loaded, 16)

            def moe_moves(l):
                if l > 0:
                    pool.wait_ge(picks_ready, l)
                pool.dma_start(w_router[:, :, 0:GROUPS], a["moe_w_group"][l].rearrange("(p k) n -> p k n", k=KD)).then_inc(router_loaded, 16)
                pool.dma_start(w_router[:, :, GROUPS:ROUTER], a["moe_w_expert"][l].rearrange("(p k) n -> p k n", k=KD)).then_inc(router_loaded, 16)
                pool.dma_start(b_router[:, 0:GROUPS], a["moe_b_group"][l:l + 1, :].partition_broadcast(P)).then_inc(router_loaded, 16)
                pool.dma_start(b_router[:, GROUPS:ROUTER], a["moe_b_expert"][l:l + 1, :].partition_broadcast(P)).then_inc(router_loaded, 16)
                pool.wait_ge(pos_ready, l + 1)
                for k in range(TOPK):
                    for t in range(TILES):
                        c = k * TILES + t
                        pool.indirect_dma_start(
                            out=xs_dram, out_offset=bass.IndirectOffsetOnAxis(ap=pos_u[:, c:c + 1], axis=0),
                            in_=h[:, t, :], in_offset=None).then_inc(scattered, 16)
                pool.wait_ge(tables_ready, l + 1)
                for j in range(2):
                    pool.dma_start(extra_t[0:1, l, j, :], extra_i[0:MAX_EXTRA, j:j + 1]).then_inc(extra_made, 16)
                pool.wait_ge(y_written, 64 * EXPERTS * (l + 1) + Y_FIRST)
                pool.wait_ge(extra_sent, l + 1)
                for t in range(TILES):
                    for k in range(TOPK):
                        c = k * TILES + t
                        pool.indirect_dma_start(
                            out=y_in[:, c, :], out_offset=None, in_=ys_dram[0:ROWS, :],
                            in_offset=bass.IndirectOffsetOnAxis(ap=pos_u[:, c:c + 1], axis=0)
                        ).then_inc(gathered[c], 16)

            def norm_scales():
                for t in range(TILES):
                    pool.wait_ge(ssq_ready, (norms[0] - 1) * TILES + t + 1)
                    step(pool.tensor_scalar(rstd[:, t:t + 1], ssq[:, t:t + 1], EPS, None, ALU.add))
                    pool.tensor_tensor(rstd[:, t:t + 1], rstd[:, t:t + 1], minus_half[:, 0:1], ALU.pow).then_inc(rstd_ready, 1)

            for ph in range(PHASES):
                if ph in stages:
                    gains(ph)
                    norm_scales()
                    if ph == 0:
                        nsa_scales()
                    if ph == 2:
                        mla_scales()
                    if ph % 2 == 1:
                        moe_moves(ph // 2)

        @block.scalar
        def _(act):
            act.sem_inc(y_written, Y_FIRST)
            norms = [0]
            turns = [0]

            def turned_half(m, t):
                act.wait_ge(h_turned, 2 * (TILES * m + t) + 1)
                nc.scalar.copy(hT[:, 0:4, t * P:(t + 1) * P],
                               ps[:, 2 * (t % 2), :].rearrange("p (k n) -> p k n", k=4)).then_inc(hT_act, 1)

            def norm_squares():
                n, m = norms[0], turns[0]
                norms[0] += 1

                def square(t):
                    if n == 0:
                        act.wait_ge(x_loaded, 16 * TILES)
                    else:
                        act.wait_ge(x_ready, TILES * n - TILES + t + 1)
                    nc.scalar.activation(h[:, t, :], x[:, t, :], ACT.Square, scale=D ** -0.5,
                                         accum_out=ssq[:, t:t + 1]).then_inc(ssq_ready, 1)

                turns[0] += 1

                def turn_copy(t):
                    turned_half(m, t)

                square(0)
                square(1)
                for t in range(2, TILES):
                    square(t)
                    turn_copy(t - 2)
                turn_copy(TILES - 2)
                turn_copy(TILES - 1)

            def moe_act(l):
                norm_squares()
                act.wait_ge(group_shift, l + 1)
                nc.scalar.activation(r8[:, 1], r8[:, 0], ACT.Exp).then_inc(group_exp, 1)
                act.wait_ge(pair_shift, l + 1)
                nc.scalar.activation(r1[:, 5], r1[:, 4], ACT.Exp).then_inc(pair_exp, 1)
                for c in range(CHUNKS):
                    act.wait_ge(chunk_turned, l * CHUNKS + c + 1)
                    nc.scalar.copy(xsT[:, 0:4, c * P:(c + 1) * P],
                                   ps[:, 2 * (c % 2), :].rearrange("p (k n) -> p k n", k=4)).then_inc(xsT_act, 1)
                base = l * EXPERTS
                act.wait_ge(tables_ready, l + 1)
                with act.Fori(0, EXPERTS // 2) as i:
                    for u in range(2):
                        done = i * 2 + (base + u)
                        row = act.value_load(start_i[0:1, l, bass.ds(i * 2 + u, 1)], min_val=0, max_val=ROWS)
                        rows = act.value_load(count_i[0:1, l, bass.ds(i * 2 + u, 1)], min_val=0, max_val=S)
                        act.wait_ge(up_done, done + 1)
                        nc.scalar.activation(silu[:, :], ps[:, 0, 0:P], ACT.Silu).then_inc(silu_done, 1)
                        act.wait_ge(hid_turned, done + 1)
                        nc.scalar.copy(hidT[:, :], ps[:, 1, 0:P]).then_inc(hidT_ready, 1)
                        act.wait_ge(y_written, done * 64 + Y_FIRST)
                        nc.scalar.nop().then_inc(y_free, 1)
                        act.wait_ge(y_ready, done + 1)
                        for half in range(2):
                            for j in range(2):
                                p0 = j * BLOCK + half * (BLOCK // 2)
                                act.dma_start(
                                    ys_dram[bass.ds(row + half * (BLOCK // 2), BLOCK // 2), j * 512:(j + 1) * 512],
                                    y_sb[p0:p0 + BLOCK // 2, u, :],
                                    cond=(rows > BLOCK // 2) if half else None).then_inc(y_written, 16)
                n = act.value_load(extra_n[0:1, l:l + 1], min_val=0, max_val=MAX_EXTRA)
                s = ex[l]
                with act.If(n > 0):
                    act.wait_ge(y_written, 64 * (base + EXPERTS) + Y_FIRST)
                    act.wait_ge(extra_made, 16 * 2 * (l + 1))
                    with act.Fori(0, n) as q:
                        row = act.value_load(extra_t[0:1, l, 1, bass.ds(q, 1)], min_val=0, max_val=ROWS)
                        act.wait_ge(s["up"], q + 1)
                        nc.scalar.activation(silu[:, :], ps[:, 0, 0:P], ACT.Silu).then_inc(s["silu"], 1)
                        act.wait_ge(s["turned"], q + 1)
                        nc.scalar.copy(hidT[:, :], ps[:, 1, 0:P]).then_inc(s["hidT"], 1)
                        act.wait_ge(s["y"], q + 1)
                        for j in range(2):
                            act.dma_start(ys_dram[bass.ds(row, BLOCK), j * 512:(j + 1) * 512],
                                          y_sb[j * BLOCK:(j + 1) * BLOCK, 0, :]).then_inc(s["written"], 16)
                        act.wait_ge(s["written"], q * 32 + 32)
                act.wait_ge(y_written, 64 * (base + EXPERTS) + Y_FIRST)
                nc.scalar.nop().then_inc(extra_sent, 1)

            def attend_act(u):
                for t in range(TILES):
                    act.wait_ge(max_done, u * TILES + (t + 1))
                    nc.scalar.activation(probs[:, t % 2, 0:(t + 1) * P], ps[:, t % 2, 0:(t + 1) * P], ACT.Exp,
                                         bias=row_max[:, t:t + 1], accum_out=row_sum[:, t:t + 1]).then_inc(exp_done, 1)

            def turn_output():
                m = turns[0]
                turns[0] += 1
                for t in range(TILES):
                    turned_half(m, t)

            def mla_act():
                norm_squares()
                for t in range(TILES):
                    act.wait_ge(c_done, t + 1)
                    if t >= 2:
                        act.wait_ge(c_turned, t - 1)
                    for j, (lo, hi) in enumerate(((0, LORA), (LORA, 2 * LORA), (2 * LORA, MLA_IN))):
                        bank = ps[:, 4 + 2 * (t % 2), lo:hi] if j < 2 else ps[:, 5 + 2 * (t % 2), 0:ROPE]
                        last = nc.scalar.activation(c_rows[:, t % 2, lo:hi], bank, ACT.Square, scale=(hi - lo) ** -0.5,
                                                    accum_out=mean_sq[:, j, t:t + 1])
                    last.then_inc(c_squares, 1)
                    if t >= 1:
                        act.wait_ge(c_turned, t)
                        nc.scalar.copy(cT[:, :, (t - 1) * P:t * P], ps[:, (t - 1) % 2, :].rearrange("p (c n) -> p c n", c=4)).then_inc(cT_ready, 1)
                t = TILES
                act.wait_ge(c_turned, t)
                nc.scalar.copy(cT[:, :, (t - 1) * P:t * P], ps[:, (t - 1) % 2, :].rearrange("p (c n) -> p c n", c=4)).then_inc(cT_ready, 1)
                act.wait_ge(kr_turned, 1)
                nc.scalar.copy(krT[0:ROPE], ps[0:ROPE, 2, :]).then_inc(krT_ready, 1)
                with act.Fori(0, HEADS) as i:
                    act.wait_ge(head_taken, i * TILES + TILES)
                    nc.scalar.activation(squares, head[:, :, 0:QK + NOPE], ACT.Square).then_inc(sq_done, 1)
                    act.wait_ge(qk_turned, i + 1)
                    nc.scalar.copy(qnT, ps[:, 7, :]).then_inc(qkT_act, 1)
                    nc.scalar.copy(qrT[0:ROPE], ps[0:ROPE, 5, :]).then_inc(qkT_act, 1)
                    attend_act(i + NSA_UNITS)
                turn_output()

            def nsa_act():
                norm_squares()
                act.wait_ge(gates_done, 1)
                nc.scalar.activation(gates[:, :, :], ps[:, 4, 0:TILES * GATES].rearrange("p (t n) -> p t n", t=TILES),
                                     ACT.Exp, scale=-1.0).then_inc(gates_exp, 1)
                act.wait_ge(bias_done, 1)
                nc.scalar.copy(cmp_bias[:, 0:1], ps[:, 5, 0:1])
                nc.scalar.copy(cmp_bias[:, 1:2], ps[:, 6, 0:1]).then_inc(bias_ready, 1)
                act.wait_ge(bias_ready, 1)
                with act.Fori(0, KV_GROUPS) as i:
                    act.wait_ge(group_taken, i * TILES + TILES)
                    nc.scalar.activation(rot_tmp, own[:, :, 0:NORMED], ACT.Square, scale=DH ** -0.5).then_inc(g_squared, 1)
                    act.wait_ge(g_turned, i + 1)
                    nc.scalar.copy(qr_pair[:, 0, :], ps[:, 4, :]).then_inc(gT_act, 1)
                    nc.scalar.copy(qr_pair[:, 1, :], ps[:, 5, :]).then_inc(gT_act, 1)
                    nc.scalar.copy(ks_low[0:DH], ps[0:DH, 0, :]).then_inc(gT_act, 1)
                    nc.scalar.copy(ks_high[DH:P], ps[0:DH, 0, :]).then_inc(gT_act, 1)
                    nc.scalar.copy(kcvT, ps[:, 1, :]).then_inc(gT_act, 1)
                    act.wait_ge(packed, i + 1)
                    nc.scalar.activation(hidden[:, 0, 0:N_CMP], ps[:, 2, 0:N_CMP], ACT.Gelu_apprx_tanh, bias=cmp_bias[:, 0:1])
                    nc.scalar.activation(hidden[:, 1, 0:N_CMP], ps[:, 3, 0:N_CMP], ACT.Gelu_apprx_tanh, bias=cmp_bias[:, 1:2]
                                         ).then_inc(gelu_done, 1)
                    act.wait_ge(cmp_made, i + 1)
                    for r in range(SHARE):
                        last = nc.scalar.copy(v_blocks[r * CMP_SLOTS:(r + 1) * CMP_SLOTS, r, :],
                                              ps[r * CMP_SLOTS:(r + 1) * CMP_SLOTS, 4, 0:DH])
                    last.then_inc(vc_ready, 1)
                    act.wait_ge(c_shifted, i + 1)
                    nc.scalar.activation(cmp_probs, cmp_probs, ACT.Exp).then_inc(c_exp, 1)
                    act.wait_ge(c_probsT, i + 1)
                    nc.scalar.copy(cmpT, ps[:, 5, :]).then_inc(c_probsT_ready, 1)
                    for j in range(UNITS):
                        attend_act(i * UNITS + j)
                turn_output()

            for ph in range(PHASES):
                if ph in stages:
                    if ph == 0:
                        nsa_act()
                    if ph == 2:
                        mla_act()
                    if ph % 2 == 1:
                        moe_act(ph // 2)

        @block.tensor
        def _(pe):
            norms = [0]

            def turn_rows(rows):
                n = norms[0]
                norms[0] += 1
                if n == 0:
                    pe.wait_ge(consts_ready, 2)
                for t in range(TILES):
                    pe.wait_ge(h_ready, n * TILES + t + 1)
                    for half in range(2):
                        if t >= 2:
                            pe.wait_ge(hT_dve if half else hT_act, n * TILES + t - 1)
                        for k in range(4):
                            last = nc.tensor.transpose(
                                ps[:, 2 * (t % 2) + half, k * P:(k + 1) * P],
                                rows[:, t, :].rearrange("p (m k) -> p k m", k=KD)[:, half * 4 + k, :], ident[:, :])
                        last.then_inc(h_turned, 1)
                pe.wait_ge(hT_act, (n + 1) * TILES)
                pe.wait_ge(hT_dve, (n + 1) * TILES)

            def expert(weights, x_rows):
                for k in range(KD):
                    for j in range(2):
                        last = nc.tensor.matmul(
                            ps[j * BLOCK:(j + 1) * BLOCK, 0, 0:2 * P].rearrange("p (g n) -> p g n", g=2), x_rows[:, k, :],
                            weights[:, 0:2, k * FF + j * P:k * FF + (j + 1) * P],
                            start=(k == 0), stop=(k == KD - 1))
                return last

            def expert_down(weights):
                for c in range(2):
                    for j in range(2):
                        last = nc.tensor.matmul(
                            ps[j * BLOCK:(j + 1) * BLOCK, 2, :], hidT[:, c * BLOCK:(c + 1) * BLOCK],
                            weights[:, 2, c * D + j * 512:c * D + (j + 1) * 512],
                            start=(c == 0), stop=(c == 1))
                return last

            def moe_pe(l):
                turn_rows(h)
                pe.wait_ge(router_loaded, 64 * (l + 1))
                for t in range(TILES):
                    for k in range(KD):
                        last = nc.tensor.matmul(ps[:, 4, t * ROUTER:(t + 1) * ROUTER], hT[:, k, t * P:(t + 1) * P],
                                                w_router[:, k, :], start=(k == 0), stop=(k == KD - 1))
                last.then_inc(logits_done, 1)
                pe.wait_ge(picks_ready, l + 1)
                for t in range(TILES):
                    for b in range(t + 1):
                        nc.tensor.matmul(ps[:, 5, t * EXPERTS:(t + 1) * EXPERTS], (below if b == t else ones)[:, :],
                                         pick[:, 2, b, :], start=(b == 0), stop=(b == t))
                for b in range(TILES):
                    last = nc.tensor.matmul(ps[:, 6, 0:EXPERTS], ones[:, :], pick[:, 2, b, :],
                                            start=(b == 0), stop=(b == TILES - 1))
                last.then_inc(counted, 1)
                for c in range(CHUNKS):
                    pe.wait_ge(chunk_loaded[c], 16 * (l + 1))
                    if c >= 2:
                        pe.wait_ge(xsT_act, l * CHUNKS + c - 1)
                        pe.wait_ge(xsT_dve, l * CHUNKS + c - 1)
                    for k in range(KD):
                        last = nc.tensor.transpose(
                            ps[:, 2 * (c % 2) + k // 4, k % 4 * P:(k % 4 + 1) * P],
                            xs_in[:, c % IN_BUFFERS, :].rearrange("p (m k) -> p k m", k=KD)[:, k, :], ident[:, :])
                    last.then_inc(chunk_turned, 1)
                pe.wait_ge(xsT_act, (l + 1) * CHUNKS)
                pe.wait_ge(xsT_dve, (l + 1) * CHUNKS)
                base = l * EXPERTS
                loads = l * (EXPERTS // SLOTS)
                with pe.Fori(0, EXPERTS // SLOTS) as i:
                    for u in range(SLOTS):
                        done = i * SLOTS + (base + u)
                        pe.wait_ge(block_ready, i * SLOTS + (base + l + u + 1))
                        pe.wait_ge(up_loaded[u], (i + (loads + 1)) * 32)
                        expert(ring[:, u], x_block[:, u % 2]).then_inc(up_done, 1)
                        pe.wait_ge(hid_done, done + 1)
                        nc.tensor.transpose(ps[:, 1, 0:P], hid[:, :], ident[:, :]).then_inc(hid_turned, 1)
                        pe.wait_ge(down_loaded[u], (i + (loads + 1)) * 16)
                        pe.wait_ge(hidT_ready, done + 1)
                        expert_down(ring[:, u]).then_inc(down_done, 1)
                s = ex[l]
                pe.wait_ge(tables_ready, l + 1)
                n = pe.value_load(extra_n[0:1, l:l + 1], min_val=0, max_val=MAX_EXTRA)
                with pe.If(n > 0):
                    with pe.Fori(0, n) as q:
                        pe.wait_ge(s["block"], q + 1)
                        pe.wait_ge(s["loaded"], q * 48 + 48)
                        expert(ring[:, 0], x_block[:, 0]).then_inc(s["up"], 1)
                        pe.wait_ge(s["hid"], q + 1)
                        nc.tensor.transpose(ps[:, 1, 0:P], hid[:, :], ident[:, :]).then_inc(s["turned"], 1)
                        pe.wait_ge(s["hidT"], q + 1)
                        pe.wait_ge(y_ready, base + EXPERTS)
                        expert_down(ring[:, 0]).then_inc(s["down"], 1)

            def attend_pe(u, parts, values, width):
                def scores(t):
                    for n, (qT, kT) in enumerate(parts):
                        last = nc.tensor.matmul(ps[:, t % 2, 0:(t + 1) * P], qT[:, t * P:(t + 1) * P],
                                                kT[:, 0:(t + 1) * P], start=(n == 0), stop=(n == len(parts) - 1))
                    last.then_inc(scores_done, 1)

                def turn_probs(t):
                    pe.wait_ge(exp_done, u * TILES + (t + 1))
                    for j in range(t + 1):
                        last = nc.tensor.transpose(ps[:, 2 + t % 2, j * P:(j + 1) * P],
                                                   probs[:, t % 2, j * P:(j + 1) * P], ident[:, :])
                    last.then_inc(probs_turned, 1)

                def weigh(t):
                    pe.wait_ge(probsT_ready, u * TILES + (t + 1))
                    if t == 0:
                        pe.wait_ge(o_taken, u + 1)
                    for j in range(t + 1):
                        last = nc.tensor.matmul(ps[:, 6, t * width:(t + 1) * width], probsT[:, t % 2, j * P:(j + 1) * P],
                                                values(j), start=(j == 0), stop=(j == t))
                    if t == TILES - 1:
                        last.then_inc(pv_done, 1)

                scores(0)
                scores(1)
                turn_probs(0)
                scores(2)
                weigh(0)
                turn_probs(1)
                scores(3)
                weigh(1)
                turn_probs(2)
                weigh(2)
                turn_probs(3)
                weigh(3)

            def project_out(w):
                turn_rows(o_rows)
                n = mixers[0]
                mixers[0] += 1
                pe.wait_ge(out_loaded, 16 * (n + 1))
                for m in range(OUT_PARTS):
                    t, half = m // 2, m % 2
                    if m >= 4:
                        pe.wait_ge(out_added, n * OUT_PARTS + m - 3)
                    for k in range(KD):
                        last = nc.tensor.matmul(ps[:, 4 + m % 4, :], hT[:, k, t * P:(t + 1) * P],
                                                w[:, k, half * 512:(half + 1) * 512], start=(k == 0), stop=(k == KD - 1))
                    last.then_inc(out_done, 1)

            mixers = [0]

            def mla_pe():
                turn_rows(h)
                pe.wait_ge(mla_in_loaded, 16)

                def turn_latents(t):
                    pe.wait_ge(c_ready, t + 1)
                    if t >= 2:
                        pe.wait_ge(cT_ready, t - 1)
                    for j in range(4):
                        last = nc.tensor.transpose(ps[:, t % 2, j * P:(j + 1) * P], c_rows[:, t % 2, j * P:(j + 1) * P], ident[:, :])
                    last.then_inc(c_turned, 1)

                for t in range(TILES):
                    if t >= 2:
                        pe.wait_ge(c_ready, t - 1)
                    for k in range(KD):
                        nc.tensor.matmul(ps[:, 4 + 2 * (t % 2), :], hT[:, k, t * P:(t + 1) * P], w_in[:, k, 0:2 * LORA],
                                         start=(k == 0), stop=(k == KD - 1))
                    for k in range(KD):
                        last = nc.tensor.matmul(ps[:, 5 + 2 * (t % 2), 0:ROPE], hT[:, k, t * P:(t + 1) * P],
                                                w_in[:, k, 2 * LORA:MLA_IN], start=(k == 0), stop=(k == KD - 1))
                    last.then_inc(c_done, 1)
                    if t >= 1:
                        turn_latents(t - 1)
                turn_latents(TILES - 1)
                pe.wait_ge(kr_staged, 1)
                for t in range(TILES):
                    last = nc.tensor.transpose(ps[0:ROPE, 2, t * P:(t + 1) * P], kr_rows[:, t, :], ident[:, :])
                last.then_inc(kr_turned, 1)
                pe.wait_ge(mla_up_loaded, 32)
                pe.wait_ge(cT_ready, TILES)
                pe.wait_ge(krT_ready, 1)
                with pe.Fori(0, HEADS) as i:
                    for t in range(TILES):
                        if t >= 2:
                            pe.wait_ge(head_taken, i * TILES + (t - 1))
                        for c in range(2):
                            nc.tensor.matmul(ps[:, 4 + t % 2, 0:QK], cT[:, c, t * P:(t + 1) * P],
                                             w_uq[:, c, bass.ds(i * QK, QK)], start=(c == 0), stop=(c == 1))
                        for c in range(2):
                            last = nc.tensor.matmul(ps[:, 4 + t % 2, QK:HEAD_COLS], cT[:, 2 + c, t * P:(t + 1) * P],
                                                    w_ukv[:, c, bass.ds(i * (NOPE + VDIM), NOPE + VDIM)],
                                                    start=(c == 0), stop=(c == 1))
                        last.then_inc(head_done, 1)
                    pe.wait_ge(qk_staged, i + 1)
                    for t in range(TILES):
                        nc.tensor.transpose(ps[:, 7, t * P:(t + 1) * P], q_rows[:, t, 0:NOPE], ident[:, :])
                        nc.tensor.transpose(ps[:, 4, t * P:(t + 1) * P], k_rows[:, t, :], ident[:, :])
                        last = nc.tensor.transpose(ps[0:ROPE, 5, t * P:(t + 1) * P], q_rows[:, t, NOPE:QK], ident[:, :])
                    last.then_inc(qk_turned, 1)
                    pe.wait_ge(qkT_act, i * 2 + 2)
                    pe.wait_ge(qkT_dve, i + 1)
                    attend_pe(i + NSA_UNITS, ((qnT, knT), (qrT[0:ROPE], krT[0:ROPE])),
                              lambda j: head[:, j, QK + NOPE:HEAD_COLS], VDIM)
                project_out(w_out)

            def nsa_pe():
                mm = nc.tensor.matmul
                turn_rows(h)
                pe.wait_ge(gates_loaded, 16)
                for t in range(TILES):
                    for k in range(KD):
                        last = mm(ps[:, 4, t * GATES:(t + 1) * GATES], hT[:, k, t * P:(t + 1) * P], w_gates[:, k, :],
                                  start=(k == 0), stop=(k == KD - 1))
                last.then_inc(gates_done, 1)
                pe.wait_ge(small_loaded, SMALL)
                pe.wait_ge(cmp_loaded, 16)
                for l in range(CMP_LEN):
                    mm(ps[:, 5, 0:1], cmp_w1[0:DH, l, :], cmp_pos[0:DH, l:l + 1], start=(l == 0), stop=(l == CMP_LEN - 1))
                    last = mm(ps[:, 6, 0:1], cmp_w1[DH:P, l, :], cmp_pos[DH:P, l:l + 1], start=(l == 0), stop=(l == CMP_LEN - 1))
                last.then_inc(bias_done, 1)
                pe.wait_ge(bias_ready, 1)
                pe.wait_ge(gates_exp, 1)
                with pe.Fori(0, KV_GROUPS) as i:
                    pe.wait_ge(group_loaded, i * 16 + 16)
                    pe.wait_ge(o_taken, i * UNITS + 1)
                    for t in range(TILES):
                        if t >= 2:
                            pe.wait_ge(group_taken, i * TILES + (t - 1))
                        b = 4 + 2 * (t % 2)
                        for k in range(KD):
                            mm(ps[:, b, :], hT[:, k, t * P:(t + 1) * P], w_group[:, k, 0:512], start=(k == 0), stop=(k == KD - 1))
                        for k in range(KD):
                            last = mm(ps[:, b + 1, 0:GROUP_IN - 512], hT[:, k, t * P:(t + 1) * P], w_group[:, k, 512:GROUP_IN],
                                      start=(k == 0), stop=(k == KD - 1))
                        last.then_inc(group_done, 1)
                    pe.wait_ge(g_staged, i + 1)
                    for t in range(TILES):
                        tt = slice(t * P, (t + 1) * P)
                        for c in range(2):
                            nc.tensor.transpose(ps[:, 4 + c, tt], qk_rot[:, t, c * P:(c + 1) * P], ident[:, :])
                            nc.tensor.transpose(ps[:, 6 + c, tt], own[:, t, c * P:(c + 1) * P], ident[:, :])
                        nc.tensor.transpose(ps[:, 0, tt], qk_rot[:, t, Q_COLS:NORMED], ident[:, :])
                        last = nc.tensor.transpose(ps[:, 1, tt], own[:, t, NORMED:NORMED + 2 * DH], ident[:, :])
                    last.then_inc(g_turned, 1)
                    pe.wait_ge(gT_act, i * 5 + 5)
                    pe.wait_ge(gT_dve, i * 4 + 4)
                    for l in range(CMP_LEN):
                        where = slice(l, l + CMP_STRIDE * (N_CMP - 1) + 1, CMP_STRIDE)
                        mm(ps[:, 2, 0:N_CMP], cmp_w1[0:DH, l, :], kcvT[0:DH, where], start=(l == 0), stop=(l == CMP_LEN - 1))
                        last = mm(ps[:, 3, 0:N_CMP], cmp_w1[DH:P, l, :], kcvT[DH:P, where], start=(l == 0), stop=(l == CMP_LEN - 1))
                    last.then_inc(packed, 1)
                    pe.wait_ge(gelu_done, i + 1)
                    for r in range(SHARE):
                        mm(ps[r * CMP_SLOTS:(r + 1) * CMP_SLOTS, 5, 0:DH], hidden[:, 0, :], cmp_w2[:, 0, :],
                           start=True, stop=True)
                        last = mm(ps[r * CMP_SLOTS:(r + 1) * CMP_SLOTS, 4, 0:DH], hidden[:, 1, :], cmp_w2[:, 1, :],
                                  start=True, stop=True)
                    last.then_inc(cmp_made, 1)
                    pe.wait_ge(kc_staged, i + 1)
                    nc.tensor.transpose(ps[:, 6, 0:P], k_cmp.rearrange("p a b -> p (a b)"), ident[:, :]).then_inc(kc_turned, 1)
                    pe.wait_ge(kc_ready, i + 1)
                    pe.wait_ge(vc_ready, i + 1)
                    for t in range(TILES):
                        for c in range(2):
                            last = mm(ps[:, 4, (t * 2 + c) * 2 * CMP_SLOTS:(t * 2 + c + 1) * 2 * CMP_SLOTS],
                                      q_pair[:, c, t * P:(t + 1) * P], k_blocks, start=True, stop=True)
                    last.then_inc(c_scored, 1)
                    pe.wait_ge(c_probs, i + 1)
                    for t in range(TILES):
                        last = nc.tensor.transpose(ps[:, 5, t * P:(t + 1) * P],
                                                   cmp_p4[:, t].rearrange("p r n -> p (r n)"), ident[:, :])
                    last.then_inc(c_probsT, 1)
                    pe.wait_ge(c_probsT_ready, i + 1)
                    for t in range(TILES):
                        last = mm(ps[:, 4 if t < 2 else 7, t % 2 * Q_COLS:(t % 2 + 1) * Q_COLS], cmpT[:, t * P:(t + 1) * P],
                                  v_blocks.rearrange("p r d -> p (r d)"), start=True, stop=True)
                    last.then_inc(c_weighed, 1)
                    for j in range(UNITS):
                        r, kind = j // 2, j % 2
                        keys = ((ks_low, ks_high), (kw_low, kw_high))[kind][r % 2]
                        attend_pe(i * UNITS + j, ((qr_pair[:, r // 2, :], keys),),
                                  lambda n, kind=kind: own[:, n, NORMED + (2 + kind) * DH:NORMED + (3 + kind) * DH], DH)
                project_out(nsa_w_out)

            for ph in range(PHASES):
                if ph in stages:
                    if ph == 0:
                        nsa_pe()
                    if ph == 2:
                        mla_pe()
                    if ph % 2 == 1:
                        moe_pe(ph // 2)

        @block.vector
        def _(dve):
            step = Chain(dve, dve_step)
            norms = [0]
            turns = [0]

            def turned_half(m, t):
                dve.wait_ge(h_turned, 2 * (TILES * m + t) + 2)
                nc.vector.tensor_copy(hT[:, 4:8, t * P:(t + 1) * P],
                                      ps[:, 2 * (t % 2) + 1, :].rearrange("p (k n) -> p k n", k=4)).then_inc(hT_dve, 1)

            dve.sem_inc(o_taken, 1)
            step(nc.vector.memset(xsT[:, :, ROWS:ROWS + BLOCK], 0.0))

            def norm(ph):
                n, m = norms[0], turns[0]
                norms[0] += 1
                turns[0] += 1

                def scale(t):
                    dve.wait_ge(rstd_ready, n * TILES + t + 1)
                    nc.vector.scalar_tensor_tensor(out=h[:, t, :], in0=x[:, t, :], scalar=rstd[:, t:t + 1],
                                                   in1=gain[:, :], op0=ALU.mult, op1=ALU.mult
                                                   ).then_inc(h_ready, 1)

                dve.wait_ge(gain_loaded, 16 * (n + 1))
                scale(0)
                for t in range(1, TILES):
                    scale(t)
                    turned_half(m, t - 1)
                nc.vector.engine_nop().then_inc(gain_used, 1)
                turned_half(m, TILES - 1)

            def first_of(values, top, eq, rank, best):
                v = nc.vector
                step(v.tensor_tensor(eq, values, top.unsqueeze(2).to_broadcast([P, TILES, 8]), ALU.is_equal))
                step(v.tensor_tensor(rank, eq, falling[:, :].unsqueeze(1).to_broadcast([P, TILES, 8]), ALU.mult))
                step(v.tensor_reduce(best, rank, AX, ALU.max))
                step(v.tensor_tensor(eq, falling[:, :].unsqueeze(1).to_broadcast([P, TILES, 8]),
                                     best.unsqueeze(2).to_broadcast([P, TILES, 8]), ALU.is_equal))

            def route(l):
                v = nc.vector
                dve.wait_ge(logits_done, l + 1)
                step(v.tensor_tensor(logit[:, :, :], ps[:, 4, 0:TILES * ROUTER].rearrange("p (t n) -> p t n", t=TILES),
                                     b_router[:, :].unsqueeze(1).to_broadcast([P, TILES, ROUTER]), ALU.add))
                lg = logit[:, :, 0:GROUPS]
                le = logit[:, :, GROUPS:ROUTER].rearrange("p t (g e) -> p t g e", g=GROUPS)
                g_top, g_sum, e_top, e_next, gap, ratio, best, share = (r1[:, i] for i in range(8))
                g_hot, rank, e_val, e_hot1, e_rest, e_hot2 = (r8[:, i] for i in range(2, 8))
                step(v.tensor_reduce(g_top, lg, AX, ALU.max))
                v.tensor_tensor(r8[:, 0], lg, g_top.unsqueeze(2).to_broadcast([P, TILES, 8]), ALU.subtract
                                ).then_inc(group_shift, 1)
                first_of(lg, g_top, g_hot, rank, best)
                step(v.tensor_tensor(pick[:, 0].rearrange("p t (g e) -> p t g e", g=GROUPS), le,
                                     g_hot.unsqueeze(3).to_broadcast([P, TILES, 8, 8]), ALU.mult))
                step(v.tensor_reduce(e_val, pick[:, 0].rearrange("p t (g e) -> p t e g", g=GROUPS), AX, ALU.add))
                step(v.tensor_reduce(e_top, e_val, AX, ALU.max))
                first_of(e_val, e_top, e_hot1, rank, best)
                step(v.scalar_tensor_tensor(out=e_rest, in0=e_hot1, scalar=NEG, in1=e_val, op0=ALU.mult, op1=ALU.add))
                step(v.tensor_reduce(e_next, e_rest, AX, ALU.max))
                v.tensor_tensor(gap, e_next, e_top, ALU.subtract).then_inc(pair_shift, 1)
                first_of(e_rest, e_next, e_hot2, rank, best)
                for k, e_hot in enumerate((e_hot1, e_hot2)):
                    step.mark(v.tensor_tensor(pick[:, k].rearrange("p t (g e) -> p t g e", g=GROUPS),
                                              g_hot.unsqueeze(3).to_broadcast([P, TILES, 8, 8]),
                                              e_hot.unsqueeze(2).to_broadcast([P, TILES, 8, 8]), ALU.mult))
                step.join()
                v.tensor_tensor(pick[:, 2], pick[:, 0], pick[:, 1], ALU.add).then_inc(picks_ready, 1)
                dve.wait_ge(group_exp, l + 1)
                step(v.tensor_reduce(g_sum, r8[:, 1], AX, ALU.add))
                dve.wait_ge(pair_exp, l + 1)
                step(v.tensor_scalar(share, ratio, 1.0, None, ALU.add))
                step(v.tensor_tensor(share, share, g_sum, ALU.mult))
                step(v.reciprocal(wt[:, 0], share))
                step(v.tensor_tensor(wt[:, 1], wt[:, 0], ratio, ALU.mult))
                dve.wait_ge(counted, l + 1)
                total, upto, start, blocks, b_upto, b_from = (count[:, i] for i in range(6))
                step(v.tensor_copy(total, ps[:, 6, 0:EXPERTS]))
                step(v.tensor_tensor_scan(upto, ones[:, 0:EXPERTS], total, 0.0, ALU.mult, ALU.add))
                step(v.tensor_tensor(start, upto, total, ALU.subtract))
                step(v.tensor_tensor(place[:, :, :], ps[:, 5, 0:TILES * EXPERTS].rearrange("p (t e) -> p t e", t=TILES),
                                     start.unsqueeze(1).to_broadcast([P, TILES, EXPERTS]), ALU.add))
                for k in range(TOPK):
                    step(v.tensor_tensor(placed[:, :, :], pick[:, k], place[:, :, :], ALU.mult))
                    step(v.tensor_reduce(pos[:, k], placed[:, :, :], AX, ALU.add))
                v.tensor_copy(pos_u[:, :], pos[:, :, :].rearrange("p k t -> p (k t)")).then_inc(pos_ready, 1)
                step.mark(v.memset(start_i[0:1, l, EXPERTS:EXPERTS + 1], 0))
                step.mark(v.tensor_copy(start_i[0:1, l, 0:EXPERTS], start[0:1, :]))
                step.mark(v.tensor_copy(count_i[0:1, l, :], total[0:1, :]))
                step(v.memset(blocks, 0.0))
                for j in range(1, S // BLOCK):
                    step(v.scalar_tensor_tensor(out=blocks, in0=total, scalar=float(j * BLOCK), in1=blocks,
                                                op0=ALU.is_gt, op1=ALU.add))
                step(v.tensor_tensor_scan(b_upto, ones[:, 0:EXPERTS], blocks, 0.0, ALU.mult, ALU.add))
                step.mark(v.tensor_copy(extra_n[0:1, l:l + 1], b_upto[0:1, EXPERTS - 1:EXPERTS]))
                step(v.tensor_tensor(b_from, b_upto, blocks, ALU.subtract))
                mine, after, row = placed[:, 0, :], placed[:, 1, :], placed[:, 2, :]
                step(v.tensor_scalar(mine, b_from, part_no[:, 0:1], None, ALU.is_le))
                step(v.tensor_scalar(after, b_upto, part_no[:, 0:1], None, ALU.is_gt))
                step(v.tensor_tensor(mine, mine, after, ALU.mult))
                step(v.scalar_tensor_tensor(out=row, in0=b_from, scalar=float(-BLOCK), in1=start, op0=ALU.mult, op1=ALU.add))
                step(v.tensor_scalar(after, part_no[:, 0:1].to_broadcast([P, EXPERTS]), float(BLOCK), float(BLOCK), ALU.mult, ALU.add))
                step(v.tensor_tensor(row, row, after, ALU.add))
                step(v.scalar_tensor_tensor(out=row, in0=upto, scalar=float(-BLOCK), in1=row, op0=ALU.add, op1=ALU.min))
                step(v.tensor_tensor(row, row, mine, ALU.mult))
                step(v.tensor_reduce(extra_f[:, 1:2], row, AX, ALU.add))
                step(v.tensor_tensor(row, mine, expert_no[:, :], ALU.mult))
                step(v.tensor_reduce(extra_f[:, 0:1], row, AX, ALU.add))
                v.tensor_copy(extra_i[:, :], extra_f[:, 0:2]).then_inc(tables_ready, 1)

            def moe_dve(l):
                norm(2 * l + 1)
                route(l)
                for c in range(CHUNKS):
                    dve.wait_ge(chunk_turned, l * CHUNKS + c + 1)
                    nc.vector.tensor_copy(xsT[:, 4:8, c * P:(c + 1) * P],
                                          ps[:, 2 * (c % 2) + 1, :].rearrange("p (k n) -> p k n", k=4)).then_inc(xsT_dve, 1)

                def take_block(where, buffer):
                    return nc.vector.tensor_copy(x_block[:, buffer], xsT[:, :, bass.ds(where, BLOCK)])

                base = l * EXPERTS
                dve.wait_ge(tables_ready, l + 1)
                dve.wait_ge(xsT_act, (l + 1) * CHUNKS)
                dve.wait_ge(xsT_dve, (l + 1) * CHUNKS)
                r = dve.value_load(start_i[0:1, l, 0:1], min_val=0, max_val=ROWS)
                take_block(r, 0).then_inc(block_ready, 1)
                with dve.Fori(0, EXPERTS // 2) as i:
                    for u in range(2):
                        done = i * 2 + (base + u)
                        dve.wait_ge(silu_done, done + 1)
                        nc.vector.tensor_tensor(hid[:, :], silu[:, :], ps[:, 0, P:2 * P], ALU.mult).then_inc(hid_done, 1)
                        r = dve.value_load(start_i[0:1, l, bass.ds(i * 2 + (u + 1), 1)], min_val=0, max_val=ROWS)
                        take_block(r, (u + 1) % 2).then_inc(block_ready, 1)
                        dve.wait_ge(down_done, done + 1)
                        dve.wait_ge(y_free, done + 1)
                        nc.vector.tensor_copy(y_sb[:, u, :], ps[:, 2, :]).then_inc(y_ready, 1)
                s = ex[l]
                n = dve.value_load(extra_n[0:1, l:l + 1], min_val=0, max_val=MAX_EXTRA)
                with dve.If(n > 0):
                    dve.wait_ge(y_written, 64 * (base + EXPERTS) + Y_FIRST)
                    dve.wait_ge(extra_made, 16 * 2 * (l + 1))
                    dve.wait_ge(block_ready, (EXPERTS + 1) * (l + 1))
                    with dve.Fori(0, n) as q:
                        r = dve.value_load(extra_t[0:1, l, 1, bass.ds(q, 1)], min_val=0, max_val=ROWS)
                        take_block(r, 0).then_inc(s["block"], 1)
                        dve.wait_ge(s["silu"], q + 1)
                        nc.vector.tensor_tensor(hid[:, :], silu[:, :], ps[:, 0, P:2 * P], ALU.mult).then_inc(s["hid"], 1)
                        dve.wait_ge(s["down"], q + 2)
                        nc.vector.tensor_copy(y_sb[:, 0, :], ps[:, 2, :]).then_inc(s["y"], 1)
                for t in range(TILES):
                    for k in range(TOPK):
                        c = k * TILES + t
                        dve.wait_ge(gathered[c], 16 * (l + 1))
                        add = nc.vector.scalar_tensor_tensor(out=x[:, t, :], in0=y_in[:, c, :], scalar=wt[:, k, t:t + 1],
                                                             in1=x[:, t, :], op0=ALU.mult, op1=ALU.add)
                        if k < TOPK - 1:
                            step(add)
                    add.then_inc(x_ready, 1)

            def attend_dve(u):
                def top(t):
                    dve.wait_ge(scores_done, u * TILES + (t + 1))
                    step(nc.vector.tensor_tensor(ps[:, t % 2, t * P:(t + 1) * P], ps[:, t % 2, t * P:(t + 1) * P],
                                                tri[:, :], ALU.add))
                    nc.vector.tensor_reduce(row_max[:, t:t + 1], ps[:, t % 2, 0:(t + 1) * P], AX, ALU.max,
                                            negate=True).then_inc(max_done, 1)

                def take(t):
                    dve.wait_ge(probs_turned, u * TILES + (t + 1))
                    nc.vector.tensor_copy(probsT[:, t % 2, 0:(t + 1) * P], ps[:, 2 + t % 2, 0:(t + 1) * P]
                                          ).then_inc(probsT_ready, 1)

                top(0)
                top(1)
                take(0)
                top(2)
                take(1)
                top(3)
                take(2)
                take(3)
                dve.wait_ge(exp_done, u * TILES + TILES)
                step(nc.vector.reciprocal(row_inv[:, :], row_sum[:, :]))
                dve.wait_ge(pv_done, u + 1)

            def add_output():
                m, n = turns[0], mixers[0]
                turns[0] += 1
                mixers[0] += 1
                for t in range(TILES):
                    turned_half(m, t)
                for part in range(OUT_PARTS):
                    t, half = part // 2, part % 2
                    dve.wait_ge(out_done, n * OUT_PARTS + part + 1)
                    add = nc.vector.tensor_tensor(x[:, t, half * 512:(half + 1) * 512], x[:, t, half * 512:(half + 1) * 512],
                                                  ps[:, 4 + part % 4, :], ALU.add)
                    add.then_inc(out_added, 1)
                    if half:
                        dve.wait_ge(out_added, n * OUT_PARTS + part + 1)
                        nc.vector.engine_nop().then_inc(x_ready, 1)

            mixers = [0]

            def rotate(rows, heads, first, second, to=None):
                v = nc.vector
                half = ROPE // 2

                def table(i, lo, hi):
                    w = turn[:, i, :, lo:hi]
                    return w.unsqueeze(2).to_broadcast([P, TILES, heads, hi - lo]) if heads else w

                def part(r, lo, hi):
                    return r[:, :, :, lo:hi] if heads else r[:, :, lo:hi]

                step.mark(v.tensor_tensor(first, rows, table(0, 0, ROPE), ALU.mult))
                step.mark(v.tensor_tensor(part(second, 0, half), part(rows, half, ROPE), table(1, 0, half), ALU.mult))
                step.mark(v.tensor_tensor(part(second, half, ROPE), part(rows, 0, half), table(1, half, ROPE), ALU.mult))
                step.join()
                return v.tensor_tensor(rows if to is None else to, first, second, ALU.add)

            def mla_dve():
                v = nc.vector
                norm(2)
                g_lat = mla_gain[:, 0:2 * LORA]
                g_qn = mla_gain[:, 2 * LORA:2 * LORA + NOPE]
                g_qr = mla_gain[:, 2 * LORA + NOPE:2 * LORA + QK]
                g_kn = mla_gain[:, 2 * LORA + QK:2 * LORA + QK + NOPE]
                g_kr = mla_gain[:, 2 * LORA + QK + NOPE:2 * LORA + 2 * QK]
                dve.wait_ge(small_loaded, SMALL)
                step(v.scalar_tensor_tensor(out=g_qn, in0=g_qn, scalar=MLA_SCALE, in1=g_kn, op0=ALU.mult, op1=ALU.mult))
                step(v.tensor_scalar(g_qr, g_qr, MLA_SCALE, None, ALU.mult))
                for t in range(TILES):
                    dve.wait_ge(c_scales, t + 1)
                    for j, (lo, hi) in enumerate(((0, LORA), (LORA, 2 * LORA))):
                        step.mark(v.scalar_tensor_tensor(out=c_rows[:, t % 2, lo:hi], in0=ps[:, 4 + 2 * (t % 2), lo:hi],
                                                         scalar=mean_sq[:, j, t:t + 1], in1=g_lat[:, lo:hi],
                                                         op0=ALU.mult, op1=ALU.mult))
                    step(v.scalar_tensor_tensor(out=kr_rows[:, t, :], in0=ps[:, 5 + 2 * (t % 2), 0:ROPE],
                                                scalar=mean_sq[:, 2, t:t + 1], in1=g_kr, op0=ALU.mult, op1=ALU.mult))
                    v.engine_nop().then_inc(c_ready, 1)
                rotate(kr_rows, 0, rope_a, rope_b).then_inc(kr_staged, 1)
                dve.wait_ge(kr_staged, 1)
                with dve.Fori(0, HEADS) as i:
                    step.enter(i, MLA_STEPS)
                    for t in range(TILES):
                        dve.wait_ge(head_done, i * TILES + (t + 1))
                        v.tensor_copy(head[:, t, :], ps[:, 4 + t % 2, 0:HEAD_COLS]).then_inc(head_taken, 1)
                    dve.wait_ge(sq_done, i + 1)
                    step.mark(v.tensor_reduce(mean_sq[:, 0, :], squares[:, :, 0:NOPE], AX, ALU.add))
                    step.mark(v.tensor_reduce(mean_sq[:, 1, :], squares[:, :, QK:QK + NOPE], AX, ALU.add))
                    step.mark(v.tensor_reduce(mean_sq[:, 2, :], squares[:, :, NOPE:QK], AX, ALU.add))
                    step.join()
                    step(v.tensor_scalar(mean_sq[:, 0:2, :], mean_sq[:, 0:2, :], 1.0 / NOPE, EPS, ALU.mult, ALU.add))
                    v.tensor_scalar(mean_sq[:, 2, :], mean_sq[:, 2, :], 1.0 / ROPE, EPS, ALU.mult, ALU.add).then_inc(ms_ready, 1)
                    dve.wait_ge(rs_ready, i + 1)
                    step.mark(v.tensor_tensor(q_rows[:, :, 0:NOPE], head[:, :, 0:NOPE],
                                             mean_sq[:, 0, :].unsqueeze(2).to_broadcast([P, TILES, NOPE]), ALU.mult))
                    step.mark(v.tensor_tensor(q_rows[:, :, NOPE:QK], head[:, :, NOPE:QK],
                                             mean_sq[:, 2, :].unsqueeze(2).to_broadcast([P, TILES, ROPE]), ALU.mult))
                    step.mark(v.tensor_tensor(k_rows, head[:, :, QK:QK + NOPE],
                                             mean_sq[:, 1, :].unsqueeze(2).to_broadcast([P, TILES, NOPE]), ALU.mult))
                    step.join()
                    step(v.tensor_tensor(q_rows, q_rows, mla_gain[:, 2 * LORA:2 * LORA + QK].unsqueeze(1
                                        ).to_broadcast([P, TILES, QK]), ALU.mult))
                    rotate(q_rows[:, :, NOPE:QK], 0, rope_a, rope_b).then_inc(qk_staged, 1)
                    dve.wait_ge(qk_turned, i + 1)
                    v.tensor_copy(knT, ps[:, 4, :]).then_inc(qkT_dve, 1)
                    attend_dve(i + NSA_UNITS)
                    v.tensor_tensor(o_rows[:, :, bass.ds(i * VDIM, VDIM)], ps[:, 6, :].rearrange("p (t n) -> p t n", t=TILES),
                                    row_inv[:, :].unsqueeze(2).to_broadcast([P, TILES, VDIM]), ALU.mult).then_inc(o_taken, 1)
                step.leave(HEADS)
                dve.wait_ge(o_taken, NSA_UNITS + HEADS + 1)
                for t in range(TILES):
                    v.engine_nop().then_inc(h_ready, 1)
                add_output()

            def nsa_dve():
                v = nc.vector
                norm(0)
                for z in (ks_low[DH:P], ks_high[0:DH], kw_low[DH:P], kw_high[0:DH], v_blocks, k_blocks, hidden):
                    step.mark(v.memset(z, 0.0))
                dve.wait_ge(small_loaded, SMALL)
                step(v.tensor_scalar(nsa_gain[:, 0:SHARE, :], nsa_gain[:, 0:SHARE, :], DH ** -0.5, None, ALU.mult))
                dve.wait_ge(gates_exp, 1)
                step(v.tensor_scalar(gates[:, :, :], gates[:, :, :], 1.0, None, ALU.add))
                step(v.reciprocal(gates[:, :, :], gates[:, :, :]))
                with dve.Fori(0, KV_GROUPS) as i:
                    step.enter(i, NSA_STEPS)
                    for t in range(TILES):
                        dve.wait_ge(group_done, i * TILES + (t + 1))
                        v.tensor_copy(own[:, t, :], ps[:, 4 + 2 * (t % 2):6 + 2 * (t % 2), :].rearrange(
                            "p b n -> p (b n)")[:, 0:GROUP_IN]).then_inc(group_taken, 1)
                    dve.wait_ge(g_squared, i + 1)
                    step(v.tensor_reduce(group_ms[:, :, :], rot_tmp.rearrange("p t (r d) -> p t r d", d=DH), AX, ALU.add))
                    v.tensor_scalar(group_ms[:, :, :], group_ms[:, :, :], EPS, None, ALU.add).then_inc(g_summed, 1)
                    dve.wait_ge(g_scales, i + 1)
                    rows = own[:, :, 0:NORMED].rearrange("p t (r d) -> p t r d", d=DH)
                    step(v.tensor_tensor(rows, rows, group_ms[:, :, :].unsqueeze(3).to_broadcast([P, TILES, SHARE + 2, DH]), ALU.mult))
                    step(v.tensor_tensor(rows, rows, nsa_gain[:, 0:SHARE + 2, :].unsqueeze(1).to_broadcast(
                        [P, TILES, SHARE + 2, DH]), ALU.mult))
                    rotate(rows, SHARE + 2, qk_rot.rearrange("p t (r d) -> p t r d", d=DH),
                           rot_tmp.rearrange("p t (r d) -> p t r d", d=DH),
                           qk_rot.rearrange("p t (r d) -> p t r d", d=DH)).then_inc(g_staged, 1)
                    dve.wait_ge(g_turned, i + 1)
                    v.tensor_copy(q_pair[:, 0, :], ps[:, 6, :]).then_inc(gT_dve, 1)
                    v.tensor_copy(q_pair[:, 1, :], ps[:, 7, :]).then_inc(gT_dve, 1)
                    v.tensor_copy(kw_low[0:DH], ps[DH:P, 0, :]).then_inc(gT_dve, 1)
                    v.tensor_copy(kw_high[DH:P], ps[DH:P, 0, :]).then_inc(gT_dve, 1)
                    dve.wait_ge(cmp_made, i + 1)
                    kc = k_cmp
                    step(v.tensor_copy(kc[:, 0, :], ps[:, 5, 0:DH]))
                    step(v.tensor_tensor(kc[:, 1, :], kc[:, 0, :], kc[:, 0, :], ALU.mult))
                    step(v.tensor_reduce(kc_ms[:, :], kc[:, 1, :], AX, ALU.add))
                    v.tensor_scalar(kc_ms[:, :], kc_ms[:, :], 1.0 / DH, EPS, ALU.mult, ALU.add
                                    ).then_inc(kc_summed, 1)
                    dve.wait_ge(kc_scale, i + 1)
                    step(v.scalar_tensor_tensor(out=kc[:, 0, :], in0=kc[:, 0, :], scalar=kc_ms[:, 0:1],
                                                in1=nsa_gain[:, SHARE + 2, :], op0=ALU.mult, op1=ALU.mult))
                    v.tensor_copy(kc[:, 1, :], kc[:, 0, :]).then_inc(kc_staged, 1)
                    dve.wait_ge(kc_turned, i + 1)
                    v.tensor_copy(k_blocks[0:DH, 0:CMP_SLOTS], ps[0:DH, 6, 0:CMP_SLOTS])
                    v.tensor_copy(k_blocks[DH:P, CMP_SLOTS:2 * CMP_SLOTS], ps[DH:P, 6, 0:CMP_SLOTS]).then_inc(kc_ready, 1)
                    dve.wait_ge(c_scored, i + 1)
                    bc = [P, TILES, SHARE, CMP_SLOTS]
                    step(v.tensor_tensor(cmp_p4, ps[:, 4, :].rearrange("p (t r n) -> p t r n", t=TILES, r=SHARE),
                                         cmp_mask[:, 0].unsqueeze(2).to_broadcast(bc), ALU.add))
                    step(v.tensor_reduce(c_max[:, :], cmp_probs, AX, ALU.max))
                    v.tensor_tensor(cmp_probs, cmp_probs, c_max[:, :].unsqueeze(2).to_broadcast([P, TILES * SHARE, CMP_SLOTS]),
                                    ALU.subtract).then_inc(c_shifted, 1)
                    dve.wait_ge(c_exp, i + 1)
                    v.tensor_tensor(cmp_p4, cmp_p4, cmp_mask[:, 1].unsqueeze(2).to_broadcast(bc), ALU.mult).then_inc(c_probs, 1)
                    dve.wait_ge(c_probs, i + 1)
                    step(v.tensor_reduce(c_sum[:, :], cmp_probs, AX, ALU.add))
                    step(v.tensor_scalar(c_sum[:, :], c_sum[:, :], 1e-30, None, ALU.max))
                    step(v.reciprocal(c_sum[:, :], c_sum[:, :]))
                    step(v.tensor_tensor(c_sum[:, :].rearrange("p (t r) -> p t r", t=TILES), c_sum[:, :].rearrange("p (t r) -> p t r", t=TILES),
                                         gates[:, :, bass.ds(i * SHARE, SHARE)], ALU.mult))
                    dve.wait_ge(c_weighed, i + 1)
                    for half in range(2):
                        last = v.tensor_tensor(
                            o_rows[:, 2 * half:2 * half + 2, bass.ds(i * Q_COLS, Q_COLS)].rearrange("p t (r d) -> p t r d", r=SHARE),
                            ps[:, 7 if half else 4, :].rearrange("p (t r d) -> p t r d", t=2, r=SHARE),
                            c_sum[:, :].rearrange("p (t r) -> p t r", t=TILES)[:, 2 * half:2 * half + 2].unsqueeze(3).to_broadcast(
                                [P, 2, SHARE, DH]), ALU.mult)
                        step.mark(last)
                    step.join()
                    for j in range(UNITS):
                        r, kind = j // 2, j % 2
                        u = i * UNITS + j
                        attend_dve(u)
                        step(v.tensor_tensor(weight[:, :].unsqueeze(2), row_inv[:, :].unsqueeze(2),
                                             gates[:, :, bass.ds(i * SHARE + ((1 + kind) * NSA_HEADS + r), 1)], ALU.mult))
                        dve.wait_ge(o_taken, u + 1)
                        for t in range(TILES):
                            cols = o_rows[:, t, bass.ds(i * Q_COLS + r * DH, DH)]
                            last = v.scalar_tensor_tensor(out=cols, in0=ps[:, 6, t * DH:(t + 1) * DH], scalar=weight[:, t:t + 1],
                                                          in1=cols, op0=ALU.mult, op1=ALU.add)
                        last.then_inc(o_taken, 1)
                step.leave(KV_GROUPS)
                dve.wait_ge(o_taken, KV_GROUPS * UNITS + 1)
                for t in range(TILES):
                    v.engine_nop().then_inc(h_ready, 1)
                add_output()

            for ph in range(PHASES):
                if ph in stages:
                    if ph == 0:
                        nsa_dve()
                    if ph == 2:
                        mla_dve()
                    if ph % 2 == 1:
                        moe_dve(ph // 2)


def layout(inputs):
    arrays = {}
    for name, value in inputs.items():
        v = np.asarray(value)
        if name == "x":
            arrays[name] = v[0]
        elif name in ("norm_mix", "norm_ffn") or name.startswith("moe_"):
            arrays[name] = v
        elif name == "nsa_w_in":
            w = v[0].reshape(P, KD, -1)
            q = w[:, :, 0:D].reshape(P, KD, KV_GROUPS, Q_COLS)
            kv = w[:, :, D:D + 6 * KV_GROUPS * DH].reshape(P, KD, 6, KV_GROUPS, DH)
            order = [q] + [kv[:, :, i] for i in (2, 4, 0, 1, 3, 5)]
            arrays["nsa_w_group"] = np.concatenate(order, axis=3).transpose(2, 0, 1, 3)
            arrays["nsa_w_gates"] = w[:, :, D + 6 * KV_GROUPS * DH:]
        elif name == "nsa_cmp_w1":
            arrays[name] = v[0].reshape(2, CMP_LEN, DH, CMP_HIDDEN).transpose(0, 2, 1, 3).reshape(P, CMP_LEN, CMP_HIDDEN)
        elif name == "nsa_cmp_pos":
            arrays[name] = v[0].transpose(0, 2, 1).reshape(P, CMP_LEN)
        elif name == "nsa_cmp_w2":
            arrays[name] = v[0].transpose(1, 0, 2)
        elif name == "nsa_k_norm":
            for i in range(3):
                arrays[f"nsa_k_norm_{i}"] = v[0, i:i + 1]
        elif name == "nsa_q_norm":
            arrays[name] = v
        elif name == "nsa_w_out":
            arrays[name] = v[0]
        elif name.startswith("mla_w"):
            arrays[name] = v[0]
        elif name.startswith("mla_"):
            arrays[name] = v
    inv = (1.0 / (np.float32(10000.0) ** (np.arange(0, ROPE, 2, dtype=np.float32) / np.float32(ROPE)))).astype(np.float32)
    angle = np.arange(S, dtype=np.float32)[:, None] * inv[None, :]
    cos, sin = np.cos(angle), np.sin(angle)
    rope = np.stack([np.concatenate([cos, cos], 1), np.concatenate([-sin, sin], 1)]).astype(np.float32)
    arrays["rope"] = rope.reshape(2, TILES, P, ROPE).transpose(2, 0, 1, 3)
    ends = np.arange(CMP_SLOTS) * CMP_STRIDE + CMP_LEN - 1
    seen = (ends[None, :] <= np.arange(S)[:, None]) & (np.arange(CMP_SLOTS)[None, :] < N_CMP)
    mask = np.stack([np.where(seen, 0.0, NEG), seen]).astype(np.float32)
    arrays["cmp_mask"] = mask.reshape(2, TILES, P, CMP_SLOTS).transpose(2, 0, 1, 3)
    return {n: np.ascontiguousarray(v) for n, v in arrays.items()}


def kernel(**inputs):
    import concourse.bacc as bacc
    from concourse.bass_utils import run_bass_kernel_spmd

    nc = bacc.Bacc("TRN2", target_bir_lowering=False, num_devices=1)
    arrays = layout(inputs)
    aps = {n: nc.dram_tensor(n, v.shape, mybir.dt.from_np(v.dtype), kind="ExternalInput").ap() for n, v in arrays.items()}
    out = nc.dram_tensor("result", (S, D), F32, kind="ExternalOutput").ap()
    build(nc, aps, out, [0, 1, 2, 3])
    r = run_bass_kernel_spmd(nc, [arrays], core_ids=[0])
    return r.results[0]["result"].reshape(1, S, D)
```

```python
from contextlib import ExitStack

import numpy as np

import concourse.bass as bass
from concourse import mybir

F32 = mybir.dt.float32
I32 = mybir.dt.int32
U32 = mybir.dt.uint32
ALU = mybir.AluOpType
ACT = mybir.ActivationFunctionType
AX = mybir.AxisListType.X

P = 128
D = 1024
S = 512
TILES = S // P
KD = D // P
LAYERS = 2
EPS = 1e-6
NEG = -1e30

GROUPS = 8
PER_GROUP = 8
EXPERTS = GROUPS * PER_GROUP
ROUTER = GROUPS + EXPERTS
TOPK = 2
FF = 256
ROWS = S * TOPK
CHUNKS = ROWS // P
BLOCK = 64
SLOTS = 4
IN_BUFFERS = 3
MAX_EXTRA = ROWS // BLOCK

KV_GROUPS = 4
SHARE = 4
NSA_HEADS = KV_GROUPS * SHARE
DH = 64
CMP_LEN = 32
CMP_STRIDE = 16
N_CMP = S // CMP_STRIDE - 1
CMP_SLOTS = 32
CMP_HIDDEN = 128
GROUP_IN = (SHARE + 6) * DH
Q_COLS = SHARE * DH
NORMED = Q_COLS + 2 * DH
GATES = 3 * NSA_HEADS
UNITS = 2 * SHARE

HEADS = 8
NOPE = 128
ROPE = 64
QK = NOPE + ROPE
VDIM = 128
LORA = 256
MLA_IN = 2 * LORA + ROPE
HEAD_COLS = QK + NOPE + VDIM
MLA_SCALE = QK ** -0.5


class Chain:

    def __init__(self, engine, semaphore):
        self.engine, self.semaphore, self.count, self.turn = engine, semaphore, 0, None

    def value(self):
        if self.turn is None:
            return self.count
        return self.turn * self.each + self.count

    def __call__(self, instruction):
        self.mark(instruction)
        self.join()

    def enter(self, turn, each):
        self.turn, self.each, self.before = turn, each, self.count

    def leave(self, turns):
        assert self.count - self.before == self.each, (self.count - self.before, self.each)
        self.turn = None
        self.count = self.before + turns * self.each

    def mark(self, instruction):
        self.count = self.count + 1
        instruction.then_inc(self.semaphore, 1)

    def join(self):
        self.engine.wait_ge(self.semaphore, self.value())


def build(nc, a, out, stages):
    with ExitStack() as ctx:
        def sb(name, shape, dt=F32):
            return ctx.enter_context(nc.sbuf_tensor("sb_" + name, shape, dt))

        def sem(name):
            return ctx.enter_context(nc.semaphore(name))

        ps = ctx.enter_context(nc.psum_tensor("ps", [P, 8, 512], F32))

        x = sb("x_res", [P, TILES, D])
        h = sb("h_norm", [P, TILES, D])
        hT = sb("hT", [P, KD, S])
        gain = sb("gain", [P, D])
        ssq = sb("ssq", [P, TILES])
        rstd = sb("rstd", [P, TILES])
        ident = sb("ident", [P, P])
        minus_half = sb("minus_half", [P, 1])
        ring = sb("ring", [P, SLOTS, 3, KD * FF])
        xsT = sb("xsT", [P, KD, ROWS + BLOCK])
        x_block = sb("x_block", [P, 2, KD, BLOCK])
        silu = sb("silu", [P, P])
        hid = sb("hid", [P, P])
        hidT = sb("hidT", [P, P])
        y_sb = sb("y_sb", [P, 2, 512])
        w_router = sb("w_router", [P, KD, ROUTER])
        b_router = sb("b_router", [P, ROUTER])
        ones = sb("ones", [P, P])
        below = sb("below", [P, P])
        falling = sb("falling", [P, 8])
        expert_no = sb("expert_no", [P, EXPERTS])
        part_no = sb("part_no", [P, 1])
        y_flat = y_sb[:, :, :].rearrange("p b n -> p (b n)")
        logit = y_flat[:, 0:TILES * ROUTER].rearrange("p (t n) -> p t n", t=TILES)
        r8 = y_flat[:, 288:544].rearrange("p (i t n) -> p i t n", i=8, t=TILES)
        placed = y_flat[:, 544:800].rearrange("p (t e) -> p t e", t=TILES)
        r1 = sb("r1", [P, 8, TILES])
        pos = sb("pos", [P, TOPK, TILES])
        pos_u = sb("pos_u", [P, TOPK * TILES], U32)
        wt = sb("wt", [P, TOPK, TILES])
        count = sb("count", [P, 6, EXPERTS])
        start_i = sb("start_i", [1, LAYERS, EXPERTS + 2], I32)
        count_i = sb("count_i", [1, LAYERS, EXPERTS], I32)
        extra_f = sb("extra_f", [P, 8])
        extra_i = sb("extra_i", [P, 2], I32)
        extra_n = sb("extra_n", [1, LAYERS], I32)
        extra_t = sb("extra_t", [1, LAYERS, 2, MAX_EXTRA], I32)
        row_of = sb("row_of", [P, EXPERTS], U32)
        row_now = sb("row_now", [P, 2], U32)
        block_token = sb("block_token", [P, 1])
        block_half = sb("block_half", [P, 1])
        xs_in = hT[:, 0:2 * IN_BUFFERS, :].rearrange("p (b j) n -> p b (j n)", b=IN_BUFFERS)
        pick = hT[:, 6:8, :].rearrange("p k n -> p (k n)")[:, 0:3 * TILES * EXPERTS].rearrange(
            "p (i t e) -> p i t e", i=3, t=TILES)
        place = hT[:, 7, S - TILES * EXPERTS:S].rearrange("p (t e) -> p t e", t=TILES)
        y_in = xsT[:, :, :].rearrange("p k n -> p (k n)")[:, 0:TOPK * TILES * D].rearrange(
            "p (b n) -> p b n", b=TOPK * TILES)

        xs_dram = nc.dram_tensor("sorted_rows", (ROWS, D), F32, kind="Internal").ap()
        ys_dram = nc.dram_tensor("expert_rows", (ROWS, D), F32, kind="Internal").ap()

        work = ring[:, 1:SLOTS].rearrange("p s i n -> p (s i n)")
        scratch = xsT[:, :, :].rearrange("p k n -> p (k n)")
        h_space = h[:, :, :].rearrange("p t n -> p (t n)")
        hT_space = hT[:, :, :].rearrange("p k n -> p (k n)")
        o_rows = scratch[:, 0:TILES * D].rearrange("p (t n) -> p t n", t=TILES)
        probs = x_block[:, :, :, :].rearrange("p b k n -> p b (k n)")
        probsT = y_sb
        row_max = sb("row_max", [P, 2 * TILES])
        row_sum = sb("row_sum", [P, 2 * TILES])
        row_inv = sb("row_inv", [P, TILES])
        tri = sb("tri", [P, P])
        turn = sb("turn", [P, 2, TILES, ROPE])

        def cut(space, at, *shape):
            size = int(np.prod(shape))
            v = space[:, at:at + size]
            if len(shape) == 2:
                v = v.rearrange("p (a b) -> p a b", a=shape[0])
            if len(shape) == 3:
                v = v.rearrange("p (a b c) -> p a b c", a=shape[0], b=shape[1])
            return v, at + size

        mla_gain = sb("mla_gain", [P, 2 * LORA + 2 * QK])
        mean_sq = sb("mean_sq", [P, 3, TILES])
        w_uq, at = cut(work, 0, 2, HEADS * QK)
        w_ukv, at = cut(work, at, 2, HEADS * (NOPE + VDIM))
        w_out, end = cut(work, at, KD, D)
        w_in, _ = cut(work, at, KD, MLA_IN)
        head, at = cut(work, end, TILES, QK + NOPE)
        q_rows, at = cut(work, at, TILES, QK)
        k_rows, at = cut(work, at, TILES, NOPE)
        squares, at = cut(scratch, TILES * D, TILES, QK + NOPE)
        rope_a, at = cut(scratch, at, TILES, ROPE)
        rope_b, at = cut(scratch, at, TILES, ROPE)
        v_rows, at = cut(scratch, at, 2 * TILES, VDIM)
        c_rows, at = cut(h_space, 0, 2, MLA_IN)
        cT, at = cut(h_space, at, 4, S)
        kr_rows, at = cut(h_space, at, TILES, ROPE)
        qnT, at = cut(hT_space, 0, S)
        knT, at = cut(hT_space, at, S)
        qrT, at = cut(hT_space, at, S)
        krT, at = cut(hT_space, at, S)

        nsa_w_out, _ = cut(work, 0, KD, D)
        w_group, at = cut(work, 0, KD, GROUP_IN)
        w_gates, at = cut(work, at, KD, GATES)
        own, at = cut(work, KD * D, TILES, GROUP_IN)
        qk_rot, at = cut(work, at, TILES, NORMED)
        spare, at = cut(work, at, 4 * S)
        ks_low, at = cut(work, at, S)
        ks_high, at = cut(work, at, S)
        kw_low, at = cut(work, at, S)
        kw_high, at = cut(work, at, S)
        rot_tmp = spare[:, 0:TILES * NORMED].rearrange("p (t n) -> p t n", t=TILES)
        kcv_pair = spare[:, 0:2 * S].rearrange("p (a n) -> p a n", a=2)
        cmpT = spare[:, 0:S]
        cmp_out = spare[:, 2 * S:4 * S].rearrange("p (t r d) -> p t r d", t=TILES, r=SHARE)
        q_pair, at = cut(scratch, TILES * D, 2, S)
        qr_pair, at = cut(scratch, at, 2, S)
        v_blocks, at = cut(scratch, at, SHARE, DH)
        k_blocks, at = cut(scratch, at, 2 * CMP_SLOTS)
        cmp_probs, at = cut(scratch, at, TILES * SHARE, CMP_SLOTS)
        cmp_p4 = cmp_probs.rearrange("p (t r) n -> p t r n", t=TILES)
        hidden, at = cut(scratch, at, 2, CMP_SLOTS)
        k_cmp, at = cut(scratch, at, 2, DH)
        cmp_w1 = h_space.rearrange("p (a m n) -> p a m n", a=2, m=CMP_LEN // 2)
        cmp_bias = sb("cmp_bias", [P, 2])
        at = KD * D + TILES * (GROUP_IN + NORMED) + 8 * S
        cmp_w2, at = cut(work, at, 2, DH)
        cmp_pos, at = cut(work, at, 2, CMP_LEN // 2)
        cmp_mask, at = cut(work, at, 2, TILES, CMP_SLOTS)
        nsa_gain, at = cut(work, at, SHARE + 3, DH)
        gates, at = cut(work, at, TILES, GATES)
        group_ms = sb("group_ms", [P, TILES, SHARE + 2])
        weight = sb("weight", [P, TILES])
        kc_ms = sb("kc_ms", [P, 1])
        c_max = sb("c_max", [P, TILES * SHARE])
        c_sum = sb("c_sum", [P, TILES * SHARE])

        group_loaded = sem("group_loaded")
        gates_loaded = sem("gates_loaded")
        cmp_loaded = sem("cmp_loaded")
        gates_done = sem("gates_done")
        gates_exp = sem("gates_exp")
        gates_taken = sem("gates_taken")
        bias_done = sem("bias_done")
        bias_ready = sem("bias_ready")
        group_done = sem("group_done")
        group_taken = sem("group_taken")
        g_squared = sem("g_squared")
        g_summed = sem("g_summed")
        g_scales = sem("g_scales")
        g_staged = sem("g_staged")
        g_turned = sem("g_turned")
        gT_act = sem("gT_act")
        gT_dve = sem("gT_dve")
        packed = sem("packed")
        gelu_done = sem("gelu_done")
        cmp_made = sem("cmp_made")
        kc_summed = sem("kc_summed")
        kc_scale = sem("kc_scale")
        kc_staged = sem("kc_staged")
        kc_turned = sem("kc_turned")
        c_added = sem("c_added")
        kc_ready = sem("kc_ready")
        vc_ready = sem("vc_ready")
        c_scored = sem("c_scored")
        c_shifted = sem("c_shifted")
        c_exp = sem("c_exp")
        c_probs = sem("c_probs")
        c_probsT = sem("c_probsT")
        c_probsT_ready = sem("c_probsT_ready")
        c_weighed = sem("c_weighed")
        small_loaded = sem("small_loaded")
        mla_gain_ready = sem("mla_gain_ready")
        mla_in_loaded = sem("mla_in_loaded")
        mla_up_loaded = sem("mla_up_loaded")
        out_loaded = sem("out_loaded")
        c_done = sem("c_done")
        c_squares = sem("c_squares")
        c_scales = sem("c_scales")
        c_ready = sem("c_ready")
        c_turned = sem("c_turned")
        cT_ready = sem("cT_ready")
        kr_staged = sem("kr_staged")
        kr_turned = sem("kr_turned")
        krT_ready = sem("krT_ready")
        head_done = sem("head_done")
        head_taken = sem("head_taken")
        sq_done = sem("sq_done")
        ms_ready = sem("ms_ready")
        rs_ready = sem("rs_ready")
        qk_staged = sem("qk_staged")
        qk_turned = sem("qk_turned")
        qkT_act = sem("qkT_act")
        qkT_dve = sem("qkT_dve")
        scores_done = sem("scores_done")
        max_done = sem("max_done")
        exp_done = sem("exp_done")
        probs_turned = sem("probs_turned")
        probsT_ready = sem("probsT_ready")
        pv_done = sem("pv_done")
        o_taken = sem("o_taken")
        out_done = sem("out_done")
        out_added = sem("out_added")
        gain_used = sem("gain_used")
        x_loaded = sem("x_loaded")
        gain_loaded = sem("gain_loaded")
        consts_ready = sem("consts_ready")
        pool_step = sem("pool_step")
        x_ready = sem("x_ready")
        ssq_ready = sem("ssq_ready")
        rstd_ready = sem("rstd_ready")
        h_ready = sem("h_ready")
        h_turned = sem("h_turned")
        hT_act = sem("hT_act")
        hT_dve = sem("hT_dve")
        dve_step = sem("dve_step")
        router_loaded = sem("router_loaded")
        logits_done = sem("logits_done")
        group_shift = sem("group_shift")
        group_exp = sem("group_exp")
        pair_shift = sem("pair_shift")
        pair_exp = sem("pair_exp")
        picks_ready = sem("picks_ready")
        counted = sem("counted")
        pos_ready = sem("pos_ready")
        tables_ready = sem("tables_ready")
        scattered = sem("scattered")
        chunk_loaded = [sem(f"chunk_loaded{i}") for i in range(CHUNKS)]
        chunk_turned = sem("chunk_turned")
        xsT_act = sem("xsT_act")
        xsT_dve = sem("xsT_dve")
        up_loaded = [sem(f"up_loaded{i}") for i in range(SLOTS)]
        down_loaded = [sem(f"down_loaded{i}") for i in range(SLOTS)]
        block_ready = sem("block_ready")
        up_done = sem("up_done")
        silu_done = sem("silu_done")
        hid_done = sem("hid_done")
        hid_turned = sem("hid_turned")
        hidT_ready = sem("hidT_ready")
        down_done = sem("down_done")
        y_ready = sem("y_ready")
        y_written = [sem(f"y_written{u}") for u in range(2)]
        y_seen = sem("y_seen")
        extra_sent = sem("extra_sent")
        extra_made = sem("extra_made")
        ex = [{n: sem(f"extra{l}_{n}") for n in
               ("loaded", "block", "up", "silu", "hid", "turned", "hidT", "down", "y", "written", "over")}
              for l in range(LAYERS)]
        gathered = [sem(f"gathered{i}") for i in range(TOPK * TILES)]
        stored = sem("stored")

        PHASES = 2 * LAYERS
        OUT_PARTS = 2 * TILES
        UP_BANKS = (0, 3)
        OUT_BANKS = 3
        NSA_UNITS = 32 if 0 in stages else 0
        MLA_STEPS = 16
        NSA_STEPS = 18 + 6 * UNITS
        SCORE_BANKS = (0, 1, 4)
        STEPS = UNITS * TILES
        AT_GELU, AT_MADE, AT_KEYS, AT_SCORE, AT_SOFT, AT_TURN, AT_WEIGH = 4, 6, 11, 13, 14, 18, 21
        SMALL = 16 * (17 if 0 in stages else 7)

        def expert_weights(eng, l, e, slot):
            gate = a["moe_w_gate"][l, e] if isinstance(e, int) else a["moe_w_gate"][l, bass.ds(e, 1)].rearrange("e k f -> (e k) f")
            up = a["moe_w_up"][l, e] if isinstance(e, int) else a["moe_w_up"][l, bass.ds(e, 1)].rearrange("e k f -> (e k) f")
            down = a["moe_w_down"][l, e] if isinstance(e, int) else a["moe_w_down"][l, bass.ds(e, 1)].rearrange("e k f -> (e k) f")
            return (
                eng.dma_start(ring[:, slot, 0, :], gate.rearrange("(p k) f -> p (k f)", k=KD)),
                eng.dma_start(ring[:, slot, 1, :], up.rearrange("(p k) f -> p (k f)", k=KD)),
                eng.dma_start(ring[:, slot, 2, :].rearrange("p (c n) -> p c n", c=FF // P),
                              down.rearrange("(c p) n -> p c n", p=P)),
            )

        block = ctx.enter_context(nc.Block())

        @block.sync
        def _(sp):
            for t in range(TILES):
                sp.dma_start(x[:, t, :], a["x"][t * P:(t + 1) * P, :]).then_inc(x_loaded, 16)

            def moe_loads(l):
                done = l * EXPERTS
                for u in range(SLOTS):
                    if l > 0 and u == 0:
                        sp.wait_ge(down_done, done)
                    if u == 1 and 2 * l in stages:
                        sp.wait_ge(out_done, OUT_PARTS * (mixers[0]))
                    g, up, dn = expert_weights(sp, l, u, u)
                    g.then_inc(up_loaded[u], 16)
                    up.then_inc(up_loaded[u], 16)
                    dn.then_inc(down_loaded[u], 16)
                sp.wait_ge(scattered, 16 * TOPK * TILES * (l + 1))
                for c in range(CHUNKS):
                    if c >= IN_BUFFERS:
                        sp.wait_ge(chunk_turned, l * CHUNKS + c - IN_BUFFERS + 1)
                    sp.dma_start(xs_in[:, c % IN_BUFFERS, :], xs_dram[c * P:(c + 1) * P, :]).then_inc(chunk_loaded[c], 16)
                with sp.Fori(1, EXPERTS // SLOTS) as i:
                    for u in range(SLOTS):
                        sp.wait_ge(down_done, (i - 1) * SLOTS + (done + u + 1))
                        g, up, dn = expert_weights(sp, l, i * SLOTS + u, u)
                        g.then_inc(up_loaded[u], 16)
                        up.then_inc(up_loaded[u], 16)
                        dn.then_inc(down_loaded[u], 16)
                sp.wait_ge(extra_made, 16 * 2 * (l + 1))
                n = sp.value_load(extra_n[0:1, l:l + 1], min_val=0, max_val=MAX_EXTRA)
                with sp.If(n > 0):
                    sp.wait_ge(down_done, done + EXPERTS)
                    sp.sem_inc(ex[l]["down"], 1)
                    with sp.Fori(0, n) as q:
                        e = sp.value_load(extra_t[0:1, l, 0, bass.ds(q, 1)], min_val=0, max_val=EXPERTS - 1)
                        sp.wait_ge(ex[l]["down"], q + 1)
                        for load in expert_weights(sp, l, e, 0):
                            load.then_inc(ex[l]["loaded"], 16)
                    sp.wait_ge(ex[l]["down"], n + 1)
                    sp.sem_inc(ex[l]["over"], 1)

            mixers = [0]

            def mla_loads():
                if 1 in stages:
                    sp.wait_ge(down_done, EXPERTS - 2)
                sp.dma_start(w_uq, a["mla_w_uq"].rearrange("(c p) n -> p c n", p=P)).then_inc(mla_up_loaded, 16)
                if 1 in stages:
                    sp.wait_ge(down_done, EXPERTS - 1)
                sp.dma_start(w_in, a["mla_w_in"].rearrange("(p k) n -> p k n", k=KD)).then_inc(mla_in_loaded, 16)
                if 1 in stages:
                    sp.wait_ge(gathered[TILES * TOPK - 1], 16)
                sp.dma_start(w_ukv, a["mla_w_ukv"].rearrange("(c p) n -> p c n", p=P)).then_inc(mla_up_loaded, 16)
                sp.wait_ge(c_done, TILES)
                mixers[0] += 1
                sp.dma_start(w_out, a["mla_w_out"].rearrange("(p k) n -> p k n", k=KD)).then_inc(out_loaded, 16)

            def nsa_loads():
                sp.dma_start(w_gates, a["nsa_w_gates"]).then_inc(gates_loaded, 16)
                sp.dma_start(w_group, a["nsa_w_group"][0]).then_inc(group_loaded, 16)
                sp.wait_ge(h_turned, 2 * TILES)
                sp.dma_start(cmp_w1, a["nsa_cmp_w1"]).then_inc(cmp_loaded, 16)
                with sp.Fori(1, KV_GROUPS) as i:
                    sp.wait_ge(group_done, i * TILES)
                    sp.dma_start(w_group, a["nsa_w_group"][bass.ds(i, 1)].rearrange("g p k n -> (g p) k n")).then_inc(group_loaded, 16)
                sp.wait_ge(group_done, KV_GROUPS * TILES)
                mixers[0] += 1
                sp.dma_start(nsa_w_out, a["nsa_w_out"].rearrange("(p k) n -> p k n", k=KD)).then_inc(out_loaded, 16)

            for ph in range(PHASES):
                if ph not in stages:
                    continue
                if ph == 0:
                    nsa_loads()
                if ph == 2:
                    mla_loads()
                if ph % 2 == 1:
                    moe_loads(ph // 2)
            sp.wait_ge(x_ready, TILES * (len(stages)))
            for t in range(TILES):
                sp.dma_start(out[t * P:(t + 1) * P, :], x[:, t, :]).then_inc(stored, 16)
            sp.wait_ge(stored, 16 * TILES)

        @block.gpsimd
        def _(pool):
            step = Chain(pool, pool_step)
            norms = [0]

            def gains(ph):
                g = a["norm_ffn"] if ph % 2 else a["norm_mix"]
                if norms[0]:
                    pool.wait_ge(gain_used, norms[0])
                norms[0] += 1
                pool.dma_start(gain[:, :], g[ph // 2:ph // 2 + 1, :].partition_broadcast(P)
                               ).then_inc(gain_loaded, 16)

            gains(stages[0])
            step(pool.memset(ones[:, :], 1.0))
            step(pool.memset(minus_half[:, :], -0.5))
            step(pool.affine_select(out=ident[:, :], in_=ones[:, :], compare_op=ALU.is_equal, fill=0.0,
                                    base=0, pattern=[[-1, P]], channel_multiplier=1))
            step(pool.affine_select(out=below[:, :], in_=ones[:, :], compare_op=ALU.is_gt, fill=0.0,
                                    base=0, pattern=[[1, P]], channel_multiplier=-1))
            step(pool.iota(falling[:, :], pattern=[[-1, 8]], base=8, channel_multiplier=0,
                           allow_small_or_imprecise_dtypes=True))
            step(pool.iota(expert_no[:, :], pattern=[[1, EXPERTS]], base=0, channel_multiplier=0,
                           allow_small_or_imprecise_dtypes=True))
            pool.iota(part_no[:, :], pattern=[[0, 1]], base=0, channel_multiplier=1,
                      allow_small_or_imprecise_dtypes=True).then_inc(consts_ready, 1)

            for j in range(2):
                step(pool.iota(block_token[j * BLOCK:(j + 1) * BLOCK, :], pattern=[[0, 1]], base=0, channel_multiplier=1,
                               allow_small_or_imprecise_dtypes=True))
                step(pool.iota(block_half[j * BLOCK:(j + 1) * BLOCK, :], pattern=[[0, 1]], base=j, channel_multiplier=2,
                               allow_small_or_imprecise_dtypes=True))
            step(pool.memset(tri[:, :], 0.0))
            pool.affine_select(out=tri[:, :], in_=tri[:, :], compare_op=ALU.is_ge, fill=NEG,
                               base=0, pattern=[[-1, P]], channel_multiplier=1).then_inc(consts_ready, 1)

            def load_router(l):
                pool.dma_start(w_router[:, :, :], a["moe_w_router"][l].rearrange("(p k) n -> p k n", k=KD)).then_inc(router_loaded, 16)
                pool.dma_start(b_router[:, :], a["moe_b_router"][l:l + 1, :].partition_broadcast(P)).then_inc(router_loaded, 16)

            pool.dma_start(turn[:, :, :, :], a["rope"]).then_inc(small_loaded, 16)
            at = 0
            for name, size in (("q_lat_norm", LORA), ("kv_lat_norm", LORA), ("q_nope_norm", NOPE),
                               ("q_rope_norm", ROPE), ("k_nope_norm", NOPE), ("k_rope_norm", ROPE)):
                pool.dma_start(mla_gain[:, at:at + size], a["mla_" + name].partition_broadcast(P)).then_inc(small_loaded, 16)
                at += size
            for i, g in enumerate(() if 0 not in stages else ("nsa_q_norm", "nsa_k_norm_1", "nsa_k_norm_2", "nsa_k_norm_0")):
                for r in (range(SHARE) if i == 0 else (SHARE + i - 1,)):
                    pool.dma_start(nsa_gain[:, r, :], a[g].partition_broadcast(P)).then_inc(small_loaded, 16)
            if 0 in stages:
                pool.dma_start(cmp_mask[:, :, :, :], a["cmp_mask"]).then_inc(small_loaded, 16)
                pool.dma_start(cmp_w2[:, :, :], a["nsa_cmp_w2"]).then_inc(small_loaded, 16)
                pool.dma_start(cmp_pos, a["nsa_cmp_pos"]).then_inc(small_loaded, 16)
            if 1 in stages:
                load_router(0)

            def nsa_scales():
                with pool.Fori(0, KV_GROUPS) as i:
                    pool.wait_ge(g_summed, i + 1)
                    pool.tensor_tensor(group_ms[:, :, :], group_ms[:, :, :],
                                       minus_half[:, 0:1].unsqueeze(1).to_broadcast([P, TILES, SHARE + 2]), ALU.pow
                                       ).then_inc(g_scales, 1)
                    pool.wait_ge(kc_summed, i + 1)
                    pool.tensor_tensor(kc_ms[:, :], kc_ms[:, :], minus_half[:, :], ALU.pow
                                       ).then_inc(kc_scale, 1)

            def mla_scales():
                c_ms = mean_sq[:, :, :]
                for t in range(TILES):
                    pool.wait_ge(c_squares, t + 1)
                    step(pool.tensor_scalar(c_ms[:, :, t], c_ms[:, :, t], EPS, None, ALU.add))
                    pool.tensor_tensor(c_ms[:, :, t], c_ms[:, :, t], minus_half[:, 0:1].to_broadcast([P, 3]),
                                       ALU.pow).then_inc(c_scales, 1)
                with pool.Fori(0, HEADS) as i:
                    pool.wait_ge(ms_ready, i + 1)
                    pool.tensor_tensor(mean_sq[:, :, :], mean_sq[:, :, :],
                                       minus_half[:, 0:1].unsqueeze(1).to_broadcast([P, 3, TILES]), ALU.pow
                                       ).then_inc(rs_ready, 1)

            def moe_moves(l):
                pool.wait_ge(pos_ready, l + 1)
                for k in range(TOPK):
                    for t in range(TILES):
                        c = k * TILES + t
                        pool.indirect_dma_start(
                            out=xs_dram, out_offset=bass.IndirectOffsetOnAxis(ap=pos_u[:, c:c + 1], axis=0),
                            in_=h[:, t, :], in_offset=None).then_inc(scattered, 16)
                pool.wait_ge(tables_ready, l + 1)
                for j in range(2):
                    pool.dma_start(extra_t[0:1, l, j, :], extra_i[0:MAX_EXTRA, j:j + 1]).then_inc(extra_made, 16)
                if l + 1 < LAYERS and 3 in stages:
                    load_router(l + 1)
                with pool.Fori(0, EXPERTS // 2) as i:
                    for u in range(2):
                        pool.wait_ge(y_ready, i * 2 + (l * EXPERTS + u + 1))
                        pool.sem_inc(y_seen, 1)
                        pool.indirect_dma_start(
                            out=ys_dram.rearrange("r (j n) -> (r j) n", j=2),
                            out_offset=bass.IndirectOffsetOnAxis(ap=row_now[:, u:u + 1], axis=0),
                            in_=y_sb[:, u, :], in_offset=None, bounds_check=2 * ROWS - 1, oob_is_err=False
                        ).then_inc(y_written[u], 16)
                for u in range(2):
                    pool.wait_ge(y_written[u], 8 * EXPERTS * (l + 1))
                pool.wait_ge(extra_sent, l + 1)
                for t in range(TILES):
                    for k in range(TOPK):
                        c = k * TILES + t
                        pool.indirect_dma_start(
                            out=y_in[:, c, :], out_offset=None, in_=ys_dram,
                            in_offset=bass.IndirectOffsetOnAxis(ap=pos_u[:, c:c + 1], axis=0)
                        ).then_inc(gathered[c], 16)

            def norm_scales(n):
                for t in range(TILES):
                    pool.wait_ge(ssq_ready, (n - 1) * TILES + t + 1)
                    step(pool.tensor_scalar(rstd[:, t:t + 1], ssq[:, t:t + 1], EPS, None, ALU.add))
                    pool.tensor_tensor(rstd[:, t:t + 1], rstd[:, t:t + 1], minus_half[:, 0:1], ALU.pow).then_inc(rstd_ready, 1)

            for ph in range(PHASES):
                if ph in stages:
                    norm_scales(norms[0])
                    later = [q for q in stages if q > ph]
                    if later:
                        gains(later[0])
                    if ph == 0:
                        nsa_scales()
                    if ph == 2:
                        mla_scales()
                    if ph % 2 == 1:
                        moe_moves(ph // 2)

        @block.scalar
        def _(act):
            norms = [0]
            turns = [0]

            def turned_half(m, t):
                act.wait_ge(h_turned, 2 * (TILES * m + t) + 1)
                nc.scalar.copy(hT[:, 0:4, t * P:(t + 1) * P],
                               ps[:, 2 * (t % 2), :].rearrange("p (k n) -> p k n", k=4)).then_inc(hT_act, 1)

            def norm_squares():
                n, m = norms[0], turns[0]
                norms[0] += 1

                def square(t):
                    if n == 0:
                        act.wait_ge(x_loaded, 16 * TILES)
                    else:
                        act.wait_ge(x_ready, TILES * n - TILES + t + 1)
                    nc.scalar.activation(h[:, t, :], x[:, t, :], ACT.Square, scale=D ** -0.5,
                                         accum_out=ssq[:, t:t + 1]).then_inc(ssq_ready, 1)

                turns[0] += 1

                def turn_copy(t):
                    turned_half(m, t)

                square(0)
                for t in range(1, TILES):
                    square(t)
                    turn_copy(t - 1)
                turn_copy(TILES - 1)

            def moe_act(l):
                norm_squares()
                act.wait_ge(group_shift, l + 1)
                nc.scalar.activation(r8[:, 1], r8[:, 0], ACT.Exp).then_inc(group_exp, 1)
                act.wait_ge(pair_shift, l + 1)
                nc.scalar.activation(r1[:, 5], r1[:, 4], ACT.Exp).then_inc(pair_exp, 1)
                for c in range(CHUNKS):
                    act.wait_ge(chunk_turned, l * CHUNKS + c + 1)
                    nc.scalar.copy(xsT[:, 0:4, c * P:(c + 1) * P],
                                   ps[:, 2 * (c % 2), :].rearrange("p (k n) -> p k n", k=4)).then_inc(xsT_act, 1)
                base = l * EXPERTS
                act.wait_ge(tables_ready, l + 1)
                nc.scalar.preload_act_table(ACT.Silu)
                with act.Fori(0, EXPERTS // 2) as i:
                    for u in range(2):
                        done = i * 2 + (base + u)
                        act.wait_ge(up_done, done + 1)
                        nc.scalar.activation(silu[:, :], ps[:, UP_BANKS[u], 0:P], ACT.Silu).then_inc(silu_done, 1)
                        act.wait_ge(hid_turned, done + 1)
                        nc.scalar.copy(hidT[:, :], ps[:, 1, 0:P]).then_inc(hidT_ready, 1)
                n = act.value_load(extra_n[0:1, l:l + 1], min_val=0, max_val=MAX_EXTRA)
                s = ex[l]
                with act.If(n > 0):
                    for u in range(2):
                        act.wait_ge(y_written[u], 8 * (base + EXPERTS))
                    act.wait_ge(extra_made, 16 * 2 * (l + 1))
                    with act.Fori(0, n) as q:
                        row = act.value_load(extra_t[0:1, l, 1, bass.ds(q, 1)], min_val=0, max_val=ROWS - BLOCK)
                        act.wait_ge(s["up"], q + 1)
                        nc.scalar.activation(silu[:, :], ps[:, 0, 0:P], ACT.Silu).then_inc(s["silu"], 1)
                        act.wait_ge(s["turned"], q + 1)
                        nc.scalar.copy(hidT[:, :], ps[:, 1, 0:P]).then_inc(s["hidT"], 1)
                        act.wait_ge(s["y"], q + 1)
                        for j in range(2):
                            act.dma_start(ys_dram[bass.ds(row, BLOCK), j * 512:(j + 1) * 512],
                                          y_sb[j * BLOCK:(j + 1) * BLOCK, 0, :]).then_inc(s["written"], 16)
                        act.wait_ge(s["written"], q * 32 + 32)
                nc.scalar.nop().then_inc(extra_sent, 1)

            def attend_act(first, steps, between, lead=None):
                def exps(s):
                    t = s % TILES
                    act.wait_ge(max_done, first + (s + 1))
                    if s >= 2:
                        act.wait_ge(probs_turned, first + (s - 1))
                    nc.scalar.activation(probs[:, s % 2, 0:(t + 1) * P], ps[:, SCORE_BANKS[s % 3], 0:(t + 1) * P], ACT.Exp,
                                         bias=row_max[:, s % 8:s % 8 + 1], accum_out=row_sum[:, s % 8:s % 8 + 1]
                                         ).then_inc(exp_done, 1)

                exps(0)
                if lead:
                    lead()
                exps(1)
                for s in range(steps):
                    t = s % TILES
                    act.wait_ge(probs_turned, first + (s + 1))
                    nc.scalar.copy(probsT[:, s % 2, 0:(t + 1) * P], ps[:, 2 + s % 2, 0:(t + 1) * P]).then_inc(probsT_ready, 1)
                    if s + 2 < steps:
                        exps(s + 2)
                    if s in between:
                        between[s]()

            def turn_output():
                m = turns[0]
                turns[0] += 1
                for t in range(TILES):
                    turned_half(m, t)

            def mla_act():
                norm_squares()
                for t in range(TILES):
                    act.wait_ge(c_done, t + 1)
                    if t >= 2:
                        act.wait_ge(c_turned, t - 1)
                    for j, (lo, hi) in enumerate(((0, LORA), (LORA, 2 * LORA), (2 * LORA, MLA_IN))):
                        bank = ps[:, 4 + 2 * (t % 2), lo:hi] if j < 2 else ps[:, 5 + 2 * (t % 2), 0:ROPE]
                        last = nc.scalar.activation(c_rows[:, t % 2, lo:hi], bank, ACT.Square, scale=(hi - lo) ** -0.5,
                                                    accum_out=mean_sq[:, j, t:t + 1])
                    last.then_inc(c_squares, 1)
                    if t >= 1:
                        act.wait_ge(c_turned, t)
                        nc.scalar.copy(cT[:, :, (t - 1) * P:t * P], ps[:, (t - 1) % 2, :].rearrange("p (c n) -> p c n", c=4)).then_inc(cT_ready, 1)
                t = TILES
                act.wait_ge(c_turned, t)
                nc.scalar.copy(cT[:, :, (t - 1) * P:t * P], ps[:, (t - 1) % 2, :].rearrange("p (c n) -> p c n", c=4)).then_inc(cT_ready, 1)
                act.wait_ge(kr_turned, 1)
                nc.scalar.copy(krT[0:ROPE], ps[0:ROPE, 2, :]).then_inc(krT_ready, 1)

                def square_head(i):
                    act.wait_ge(head_taken, i * TILES + TILES)
                    nc.scalar.activation(squares, head, ACT.Square).then_inc(sq_done, 1)

                def attend_head(i, more):
                    act.wait_ge(qk_turned, i + 1)
                    nc.scalar.copy(qnT, ps[:, 7, :]).then_inc(qkT_act, 1)
                    nc.scalar.copy(qrT[0:ROPE], ps[0:ROPE, 5, :]).then_inc(qkT_act, 1)
                    attend_act(i * TILES + NSA_UNITS * TILES, TILES, {}, (lambda: square_head(i + 1)) if more else None)

                square_head(0)
                with act.Fori(0, HEADS // 2 - 1) as i:
                    for u in range(2):
                        attend_head(i * 2 + u, True)
                attend_head(HEADS - 2, True)
                attend_head(HEADS - 1, False)
                turn_output()

            def nsa_act():
                norm_squares()
                act.wait_ge(gates_done, 1)
                nc.scalar.activation(gates[:, :, :], ps[:, 4, 0:TILES * GATES].rearrange("p (t n) -> p t n", t=TILES),
                                     ACT.Exp, scale=-1.0).then_inc(gates_exp, 1)
                act.wait_ge(bias_done, 1)
                nc.scalar.copy(cmp_bias[:, :], ps[:, 5, 0:2]).then_inc(bias_ready, 1)
                act.wait_ge(bias_ready, 1)
                with act.Fori(0, KV_GROUPS) as i:
                    act.wait_ge(group_taken, i * TILES + TILES)
                    nc.scalar.activation(rot_tmp, own[:, :, 0:NORMED], ACT.Square, scale=DH ** -0.5).then_inc(g_squared, 1)
                    act.wait_ge(g_turned, i + 1)
                    nc.scalar.copy(qr_pair[:, 0, :], ps[:, 4, :]).then_inc(gT_act, 1)
                    nc.scalar.copy(qr_pair[:, 1, :], ps[:, 5, :]).then_inc(gT_act, 1)
                    nc.scalar.copy(ks_low[0:DH], ps[0:DH, 0, :]).then_inc(gT_act, 1)
                    nc.scalar.copy(ks_high[DH:P], ps[0:DH, 0, :]).then_inc(gT_act, 1)
                    nc.scalar.copy(kcv_pair[0:DH, 0, :], ps[0:DH, 1, :]).then_inc(gT_act, 1)
                    nc.scalar.copy(kcv_pair[DH:P, 0, 0:S - 1], ps[0:DH, 1, 1:S]).then_inc(gT_act, 1)

                    def gelu():
                        act.wait_ge(packed, i + 1)
                        for a2 in range(2):
                            last = nc.scalar.activation(hidden[:, a2, 0:N_CMP], ps[:, 5, a2 * CMP_SLOTS:a2 * CMP_SLOTS + N_CMP],
                                                        ACT.Gelu_apprx_tanh, bias=cmp_bias[:, a2:a2 + 1])
                        last.then_inc(gelu_done, 1)

                    def spread_values():
                        act.wait_ge(cmp_made, i + 1)
                        for r in range(SHARE):
                            last = nc.scalar.copy(v_blocks[r * CMP_SLOTS:(r + 1) * CMP_SLOTS, r, :],
                                                  ps[r * CMP_SLOTS:(r + 1) * CMP_SLOTS, 5, 2 * DH:3 * DH])
                        last.then_inc(vc_ready, 1)

                    def cmp_exp():
                        act.wait_ge(c_shifted, i + 1)
                        nc.scalar.activation(cmp_probs, cmp_probs, ACT.Exp).then_inc(c_exp, 1)

                    def cmp_copy():
                        act.wait_ge(c_probsT, i + 1)
                        nc.scalar.copy(cmpT, ps[:, 5, :]).then_inc(c_probsT_ready, 1)

                    between = {AT_GELU: gelu, AT_MADE + 1: spread_values, AT_SOFT + 1: cmp_exp, AT_TURN + 1: cmp_copy}
                    attend_act(i * STEPS, STEPS, between)
                turn_output()

            for ph in range(PHASES):
                if ph in stages:
                    if ph == 0:
                        nsa_act()
                    if ph == 2:
                        mla_act()
                    if ph % 2 == 1:
                        moe_act(ph // 2)

        @block.tensor
        def _(pe):
            norms = [0]

            def turn_rows(rows, after=None):
                n = norms[0]
                norms[0] += 1
                if n == 0:
                    pe.wait_ge(consts_ready, 2)
                for t in range(TILES):
                    turn_tile(rows, n, t, after)
                finish_turns(n, after)

            def finish_turns(n, after):
                pe.wait_ge(hT_act, (n + 1) * TILES)
                pe.wait_ge(hT_dve, (n + 1) * TILES)
                if after:
                    after(TILES - 1)

            def turn_tile(rows, n, t, after):
                pe.wait_ge(h_ready, n * TILES + t + 1)
                for half in range(2):
                    if t >= 2:
                        pe.wait_ge(hT_dve if half else hT_act, n * TILES + t - 1)
                    for k in range(4):
                        last = nc.tensor.transpose(
                            ps[:, 2 * (t % 2) + half, k * P:(k + 1) * P],
                            rows[:, t, :].rearrange("p (m k) -> p k m", k=KD)[:, half * 4 + k, :], ident[:, :])
                    last.then_inc(h_turned, 1)
                if after and t >= 1:
                    pe.wait_ge(hT_act, n * TILES + t)
                    pe.wait_ge(hT_dve, n * TILES + t)
                    after(t - 1)

            def expert(weights, x_rows, bank):
                for k in range(KD):
                    for j in range(2):
                        last = nc.tensor.matmul(
                            ps[j * BLOCK:(j + 1) * BLOCK, bank, 0:2 * P].rearrange("p (g n) -> p g n", g=2), x_rows[:, k, :],
                            weights[:, 0:2, k * FF + j * P:k * FF + (j + 1) * P],
                            start=(k == 0), stop=(k == KD - 1))
                return last

            def expert_down(weights):
                for c in range(2):
                    for j in range(2):
                        last = nc.tensor.matmul(
                            ps[j * BLOCK:(j + 1) * BLOCK, 2, :], hidT[:, c * BLOCK:(c + 1) * BLOCK],
                            weights[:, 2, c * D + j * 512:c * D + (j + 1) * 512],
                            start=(c == 0), stop=(c == 1))
                return last

            def logits(l, t):
                if t == 0:
                    pe.wait_ge(router_loaded, 32 * (l + 1))
                for k in range(KD):
                    last = nc.tensor.matmul(ps[:, 7, t * ROUTER:(t + 1) * ROUTER], hT[:, k, t * P:(t + 1) * P],
                                            w_router[:, k, :], start=(k == 0), stop=(k == KD - 1))
                if t == TILES - 1:
                    last.then_inc(logits_done, 1)

            def moe_pe(l):
                if l * 2 not in stages:
                    turn_rows(h, lambda t: logits(l, t))
                pe.wait_ge(picks_ready, l + 1)
                for t in range(TILES):
                    for b in range(t + 1):
                        nc.tensor.matmul(ps[:, 5, t * EXPERTS:(t + 1) * EXPERTS], (below if b == t else ones)[:, :],
                                         pick[:, 2, b, :], start=(b == 0), stop=(b == t))
                for b in range(TILES):
                    last = nc.tensor.matmul(ps[:, 6, 0:EXPERTS], ones[:, :], pick[:, 2, b, :],
                                            start=(b == 0), stop=(b == TILES - 1))
                last.then_inc(counted, 1)
                for c in range(CHUNKS):
                    pe.wait_ge(chunk_loaded[c], 16 * (l + 1))
                    if c >= 2:
                        pe.wait_ge(xsT_act, l * CHUNKS + c - 1)
                        pe.wait_ge(xsT_dve, l * CHUNKS + c - 1)
                    for k in range(KD):
                        last = nc.tensor.transpose(
                            ps[:, 2 * (c % 2) + k // 4, k % 4 * P:(k % 4 + 1) * P],
                            xs_in[:, c % IN_BUFFERS, :].rearrange("p (m k) -> p k m", k=KD)[:, k, :], ident[:, :])
                    last.then_inc(chunk_turned, 1)
                pe.wait_ge(xsT_act, (l + 1) * CHUNKS)
                pe.wait_ge(xsT_dve, (l + 1) * CHUNKS)
                base = l * EXPERTS
                loads = l * (EXPERTS // SLOTS)

                def up(n, u, turn):
                    pe.wait_ge(block_ready, n + (l * (EXPERTS + 2) + 1))
                    pe.wait_ge(up_loaded[u], (turn + (loads + 1)) * 32)
                    expert(ring[:, u], x_block[:, u % 2], UP_BANKS[u % 2]).then_inc(up_done, 1)

                def down(n, u, turn):
                    pe.wait_ge(hid_done, n + (base + 1))
                    nc.tensor.transpose(ps[:, 1, 0:P], hid[:, :], ident[:, :]).then_inc(hid_turned, 1)
                    pe.wait_ge(down_loaded[u], (turn + (loads + 1)) * 16)
                    pe.wait_ge(hidT_ready, n + (base + 1))
                    expert_down(ring[:, u]).then_inc(down_done, 1)

                up(0, 0, 0)
                with pe.Fori(0, EXPERTS // SLOTS - 1) as i:
                    for u in range(SLOTS):
                        up(i * SLOTS + (u + 1), (u + 1) % SLOTS, i + (u + 1) // SLOTS)
                        down(i * SLOTS + u, u, i)
                last = EXPERTS // SLOTS - 1
                for u in range(SLOTS):
                    if u + 1 < SLOTS:
                        up(last * SLOTS + u + 1, u + 1, last)
                    down(last * SLOTS + u, u, last)
                s = ex[l]
                pe.wait_ge(tables_ready, l + 1)
                n = pe.value_load(extra_n[0:1, l:l + 1], min_val=0, max_val=MAX_EXTRA)
                with pe.If(n > 0):
                    with pe.Fori(0, n) as q:
                        pe.wait_ge(s["block"], q + 1)
                        pe.wait_ge(s["loaded"], q * 48 + 48)
                        expert(ring[:, 0], x_block[:, 0], UP_BANKS[0]).then_inc(s["up"], 1)
                        pe.wait_ge(s["hid"], q + 1)
                        nc.tensor.transpose(ps[:, 1, 0:P], hid[:, :], ident[:, :]).then_inc(s["turned"], 1)
                        pe.wait_ge(s["hidT"], q + 1)
                        pe.wait_ge(y_ready, base + EXPERTS)
                        expert_down(ring[:, 0]).then_inc(s["down"], 1)

            def attend_pe(first, head0, steps, step_of, width, between, lead=None):
                def scores(s):
                    t = s % TILES
                    parts, _ = step_of(s)
                    for n, (qT, kT) in enumerate(parts):
                        last = nc.tensor.matmul(ps[:, SCORE_BANKS[s % 3], 0:(t + 1) * P], qT[:, t * P:(t + 1) * P],
                                                kT[:, 0:(t + 1) * P], start=(n == 0), stop=(n == len(parts) - 1))
                    last.then_inc(scores_done, 1)

                def turn_probs(s):
                    pe.wait_ge(exp_done, first + (s + 1))
                    for j in range(s % TILES + 1):
                        last = nc.tensor.transpose(ps[:, 2 + s % 2, j * P:(j + 1) * P],
                                                   probs[:, s % 2, j * P:(j + 1) * P], ident[:, :])
                    last.then_inc(probs_turned, 1)

                def weigh(s):
                    t, head = s % TILES, s // TILES
                    _, values = step_of(s)
                    pe.wait_ge(probsT_ready, first + (s + 1))
                    if t == 0 and head >= 2:
                        pe.wait_ge(o_taken, head0 + (head - 1 + 1))
                    for j in range(t + 1):
                        last = nc.tensor.matmul(ps[:, 6 + head % 2, t * width:(t + 1) * width],
                                                probsT[:, s % 2, j * P:(j + 1) * P],
                                                values(j), start=(j == 0), stop=(j == t))
                    if t == TILES - 1:
                        last.then_inc(pv_done, 1)

                for s in range(3):
                    scores(s)
                    if s == 0 and lead:
                        lead()
                for s in range(steps + 1):
                    if s < steps:
                        turn_probs(s)
                    if s + 3 < steps:
                        scores(s + 3)
                    if s >= 1:
                        weigh(s - 1)
                    if s in between:
                        between[s]()

            def project_out(w, layer):
                turn_rows(o_rows)
                n = mixers[0]
                mixers[0] += 1
                pe.wait_ge(out_loaded, 16 * (n + 1))
                following = 2 * layer + 1 in stages
                after = (lambda t: logits(layer, t)) if following else None
                turn = norms[0]
                norms[0] += following
                for t in range(TILES):
                    for half in range(2):
                        m = 2 * t + half
                        if m >= OUT_BANKS:
                            pe.wait_ge(out_added, n * OUT_PARTS + m - OUT_BANKS + 1)
                        for k in range(KD):
                            last = nc.tensor.matmul(ps[:, 4 + m % OUT_BANKS, :], hT[:, k, t * P:(t + 1) * P],
                                                    w[:, k, half * 512:(half + 1) * 512], start=(k == 0), stop=(k == KD - 1))
                        last.then_inc(out_done, 1)
                    if following and t >= 1:
                        turn_tile(h, turn, t - 1, after)
                if following:
                    turn_tile(h, turn, TILES - 1, after)
                    finish_turns(turn, after)

            mixers = [0]

            def mla_pe():
                def turn_latents(t):
                    pe.wait_ge(c_ready, t + 1)
                    if t >= 2:
                        pe.wait_ge(cT_ready, t - 1)
                    for j in range(4):
                        last = nc.tensor.transpose(ps[:, t % 2, j * P:(j + 1) * P], c_rows[:, t % 2, j * P:(j + 1) * P], ident[:, :])
                    last.then_inc(c_turned, 1)

                def latents(t):
                    if t == 0:
                        pe.wait_ge(mla_in_loaded, 16)
                    if t >= 2:
                        pe.wait_ge(c_ready, t - 1)
                    for k in range(KD):
                        nc.tensor.matmul(ps[:, 4 + 2 * (t % 2), :], hT[:, k, t * P:(t + 1) * P], w_in[:, k, 0:2 * LORA],
                                         start=(k == 0), stop=(k == KD - 1))
                    for k in range(KD):
                        last = nc.tensor.matmul(ps[:, 5 + 2 * (t % 2), 0:ROPE], hT[:, k, t * P:(t + 1) * P],
                                                w_in[:, k, 2 * LORA:MLA_IN], start=(k == 0), stop=(k == KD - 1))
                    last.then_inc(c_done, 1)
                    if t == TILES - 2:
                        pe.wait_ge(hT_act, norms[0] * TILES - 1)
                        pe.wait_ge(hT_dve, norms[0] * TILES - 1)
                        turn_latents(0)
                        turn_latents(1)

                turn_rows(h, latents)
                for t in range(2, TILES):
                    turn_latents(t)
                pe.wait_ge(kr_staged, 1)
                for t in range(TILES):
                    last = nc.tensor.transpose(ps[0:ROPE, 2, t * P:(t + 1) * P], kr_rows[:, t, :], ident[:, :])
                last.then_inc(kr_turned, 1)
                pe.wait_ge(mla_up_loaded, 32)
                pe.wait_ge(cT_ready, TILES)
                pe.wait_ge(krT_ready, 1)

                def project(i, tiles):
                    for t in tiles:
                        if t >= 2:
                            pe.wait_ge(head_taken, i * TILES + (t - 1))
                        for c in range(2):
                            nc.tensor.matmul(ps[:, 2 + t % 2, 0:QK], cT[:, c, t * P:(t + 1) * P],
                                             w_uq[:, c, bass.ds(i * QK, QK)], start=(c == 0), stop=(c == 1))
                        for c in range(2):
                            last = nc.tensor.matmul(ps[:, 2 + t % 2, QK:HEAD_COLS], cT[:, 2 + c, t * P:(t + 1) * P],
                                                    w_ukv[:, c, bass.ds(i * (NOPE + VDIM), NOPE + VDIM)],
                                                    start=(c == 0), stop=(c == 1))
                        last.then_inc(head_done, 1)

                def attend_head(i, u, more):
                    pe.wait_ge(qk_staged, i + 1)
                    for t in range(TILES):
                        nc.tensor.transpose(ps[:, 7, t * P:(t + 1) * P], q_rows[:, t, 0:NOPE], ident[:, :])
                        nc.tensor.transpose(ps[:, 4, t * P:(t + 1) * P], k_rows[:, t, :], ident[:, :])
                        last = nc.tensor.transpose(ps[0:ROPE, 5, t * P:(t + 1) * P], q_rows[:, t, NOPE:QK], ident[:, :])
                    last.then_inc(qk_turned, 1)
                    if more:
                        project(i + 1, range(TILES - 1))
                    pe.wait_ge(qkT_act, i * 2 + 2)
                    pe.wait_ge(qkT_dve, i + 1)
                    pe.wait_ge(o_taken, i + (NSA_UNITS + 1))
                    attend_pe(i * TILES + NSA_UNITS * TILES, i + NSA_UNITS, TILES,
                              lambda s: (((qnT, knT), (qrT[0:ROPE], krT[0:ROPE])),
                                         lambda j: v_rows[:, u * TILES + j, :]), VDIM, {},
                              (lambda: project(i + 1, (TILES - 1,))) if more else None)

                project(0, range(TILES))
                with pe.Fori(0, HEADS // 2 - 1) as i:
                    for u in range(2):
                        attend_head(i * 2 + u, u, True)
                attend_head(HEADS - 2, 0, True)
                attend_head(HEADS - 1, 1, False)
                project_out(w_out, 1)

            def nsa_pe():
                mm = nc.tensor.matmul
                turn_rows(h)
                pe.wait_ge(gates_loaded, 16)
                for t in range(TILES):
                    for k in range(KD):
                        last = mm(ps[:, 4, t * GATES:(t + 1) * GATES], hT[:, k, t * P:(t + 1) * P], w_gates[:, k, :],
                                  start=(k == 0), stop=(k == KD - 1))
                last.then_inc(gates_done, 1)
                pe.wait_ge(small_loaded, SMALL)
                pe.wait_ge(cmp_loaded, 16)
                for a2 in range(2):
                    for m in range(CMP_LEN // 2):
                        last = mm(ps[:, 5, a2:a2 + 1], cmp_w1[:, a2, m, :], cmp_pos[:, a2, m:m + 1],
                                  start=(m == 0), stop=(m == CMP_LEN // 2 - 1))
                last.then_inc(bias_done, 1)
                pe.wait_ge(bias_ready, 1)
                pe.wait_ge(gates_exp, 1)
                with pe.Fori(0, KV_GROUPS) as i:
                    pe.wait_ge(group_loaded, i * 16 + 16)
                    pe.wait_ge(o_taken, i * UNITS + 1)
                    for t in range(TILES):
                        if t >= 2:
                            pe.wait_ge(group_taken, i * TILES + (t - 1))
                        b = 4 + 2 * (t % 2)
                        for k in range(KD):
                            mm(ps[:, b, :], hT[:, k, t * P:(t + 1) * P], w_group[:, k, 0:512], start=(k == 0), stop=(k == KD - 1))
                        for k in range(KD):
                            last = mm(ps[:, b + 1, 0:GROUP_IN - 512], hT[:, k, t * P:(t + 1) * P], w_group[:, k, 512:GROUP_IN],
                                      start=(k == 0), stop=(k == KD - 1))
                        last.then_inc(group_done, 1)
                    pe.wait_ge(g_staged, i + 1)
                    for t in range(TILES):
                        tt = slice(t * P, (t + 1) * P)
                        for c in range(2):
                            nc.tensor.transpose(ps[:, 4 + c, tt], qk_rot[:, t, c * P:(c + 1) * P], ident[:, :])
                            nc.tensor.transpose(ps[:, 6 + c, tt], own[:, t, c * P:(c + 1) * P], ident[:, :])
                        nc.tensor.transpose(ps[:, 0, tt], qk_rot[:, t, Q_COLS:NORMED], ident[:, :])
                        last = nc.tensor.transpose(ps[:, 1, tt], own[:, t, NORMED:NORMED + 2 * DH], ident[:, :])
                    last.then_inc(g_turned, 1)
                    pe.wait_ge(gT_act, i * 6 + 6)
                    pe.wait_ge(gT_dve, i * 6 + 6)

                    def pack(a2):
                        for m in range(CMP_LEN // 2):
                            where = slice(2 * m, 2 * m + CMP_STRIDE * (N_CMP - 1) + 1, CMP_STRIDE)
                            last = mm(ps[:, 5, a2 * CMP_SLOTS:a2 * CMP_SLOTS + N_CMP], cmp_w1[:, a2, m, :],
                                      kcv_pair[:, a2, where], start=(m == 0), stop=(m == CMP_LEN // 2 - 1))
                        if a2:
                            last.then_inc(packed, 1)

                    def make():
                        pe.wait_ge(gelu_done, i + 1)
                        for a2 in range(2):
                            for r in range(SHARE):
                                last = mm(ps[r * CMP_SLOTS:(r + 1) * CMP_SLOTS, 5, (1 + a2) * DH:(2 + a2) * DH],
                                          hidden[:, a2, :], cmp_w2[:, a2, :], start=True, stop=True)
                        last.then_inc(cmp_made, 1)

                    def turn_keys():
                        pe.wait_ge(kc_staged, i + 1)
                        pe.wait_ge(vc_ready, i + 1)
                        nc.tensor.transpose(ps[:, 5, 3 * P:4 * P], k_cmp.rearrange("p a b -> p (a b)"), ident[:, :]).then_inc(kc_turned, 1)

                    def cmp_scores():
                        pe.wait_ge(kc_ready, i + 1)
                        for t in range(TILES):
                            for c in range(2):
                                last = mm(ps[:, 5, (t * 2 + c) * 2 * CMP_SLOTS:(t * 2 + c + 1) * 2 * CMP_SLOTS],
                                          q_pair[:, c, t * P:(t + 1) * P], k_blocks, start=True, stop=True)
                        last.then_inc(c_scored, 1)

                    def cmp_turn():
                        pe.wait_ge(c_probs, i + 1)
                        for t in range(TILES):
                            last = nc.tensor.transpose(ps[:, 5, t * P:(t + 1) * P],
                                                       cmp_p4[:, t].rearrange("p r n -> p (r n)"), ident[:, :])
                        last.then_inc(c_probsT, 1)

                    def cmp_weigh(half):
                        pe.wait_ge(c_probsT_ready, i + 1)
                        if half:
                            pe.wait_ge(c_added, i + 1)
                        for t in range(2 * half, 2 * half + 2):
                            last = mm(ps[:, 5, t % 2 * Q_COLS:(t % 2 + 1) * Q_COLS], cmpT[:, t * P:(t + 1) * P],
                                      v_blocks.rearrange("p r d -> p (r d)"), start=True, stop=True)
                        last.then_inc(c_weighed, 1)

                    between = {1: lambda: pack(0), 3: lambda: pack(1), AT_MADE: make, AT_KEYS: turn_keys, AT_SCORE: cmp_scores,
                               AT_TURN: cmp_turn, AT_WEIGH: lambda: cmp_weigh(0), AT_WEIGH + 2: lambda: cmp_weigh(1)}

                    def step_of(s):
                        j = s // TILES
                        r, kind = j // 2, j % 2
                        keys = ((ks_low, ks_high), (kw_low, kw_high))[kind][r % 2]
                        return (((qr_pair[:, r // 2, :], keys),),
                                lambda n: own[:, n, NORMED + (2 + kind) * DH:NORMED + (3 + kind) * DH])

                    attend_pe(i * STEPS, i * UNITS, STEPS, step_of, DH, between)
                project_out(nsa_w_out, 0)

            for ph in range(PHASES):
                if ph in stages:
                    if ph == 0:
                        nsa_pe()
                    if ph == 2:
                        mla_pe()
                    if ph % 2 == 1:
                        moe_pe(ph // 2)

        @block.vector
        def _(dve):
            step = Chain(dve, dve_step)
            norms = [0]
            turns = [0]

            def turned_half(m, t):
                dve.wait_ge(h_turned, 2 * (TILES * m + t) + 2)
                nc.vector.tensor_copy(hT[:, 4:8, t * P:(t + 1) * P],
                                      ps[:, 2 * (t % 2) + 1, :].rearrange("p (k n) -> p k n", k=4)).then_inc(hT_dve, 1)

            dve.sem_inc(o_taken, 1)
            step(nc.vector.memset(xsT[:, :, ROWS:ROWS + BLOCK], 0.0))

            def scale(n, t):
                if t == 0:
                    dve.wait_ge(gain_loaded, 16 * (n + 1))
                dve.wait_ge(rstd_ready, n * TILES + t + 1)
                nc.vector.scalar_tensor_tensor(out=h[:, t, :], in0=x[:, t, :], scalar=rstd[:, t:t + 1],
                                               in1=gain[:, :], op0=ALU.mult, op1=ALU.mult
                                               ).then_inc(h_ready, 1)
                if t == TILES - 1:
                    nc.vector.engine_nop().then_inc(gain_used, 1)

            def norm():
                n, m = norms[0], turns[0]
                norms[0] += 1
                turns[0] += 1
                scale(n, 0)
                for t in range(1, TILES):
                    scale(n, t)
                    turned_half(m, t - 1)
                turned_half(m, TILES - 1)

            def first_of(values, top, eq, rank, best):
                v = nc.vector
                step(v.tensor_tensor(eq, values, top.unsqueeze(2).to_broadcast([P, TILES, 8]), ALU.is_equal))
                step(v.tensor_tensor(rank, eq, falling[:, :].unsqueeze(1).to_broadcast([P, TILES, 8]), ALU.mult))
                step(v.tensor_reduce(best, rank, AX, ALU.max))
                step(v.tensor_tensor(eq, falling[:, :].unsqueeze(1).to_broadcast([P, TILES, 8]),
                                     best.unsqueeze(2).to_broadcast([P, TILES, 8]), ALU.is_equal))

            def route(l):
                v = nc.vector
                dve.wait_ge(logits_done, l + 1)
                step(v.tensor_tensor(logit[:, :, :], ps[:, 7, 0:TILES * ROUTER].rearrange("p (t n) -> p t n", t=TILES),
                                     b_router[:, :].unsqueeze(1).to_broadcast([P, TILES, ROUTER]), ALU.add))
                lg = logit[:, :, 0:GROUPS]
                le = logit[:, :, GROUPS:ROUTER].rearrange("p t (g e) -> p t g e", g=GROUPS)
                g_top, g_sum, e_top, e_next, gap, ratio, best, share = (r1[:, i] for i in range(8))
                g_hot, rank, e_val, e_hot1, e_rest, e_hot2 = (r8[:, i] for i in range(2, 8))
                step(v.tensor_reduce(g_top, lg, AX, ALU.max))
                v.tensor_tensor(r8[:, 0], lg, g_top.unsqueeze(2).to_broadcast([P, TILES, 8]), ALU.subtract
                                ).then_inc(group_shift, 1)
                first_of(lg, g_top, g_hot, rank, best)
                step(v.tensor_tensor(pick[:, 0].rearrange("p t (g e) -> p t g e", g=GROUPS), le,
                                     g_hot.unsqueeze(3).to_broadcast([P, TILES, 8, 8]), ALU.mult))
                step(v.tensor_reduce(e_val, pick[:, 0].rearrange("p t (g e) -> p t e g", g=GROUPS), AX, ALU.add))
                step(v.tensor_reduce(e_top, e_val, AX, ALU.max))
                first_of(e_val, e_top, e_hot1, rank, best)
                step(v.scalar_tensor_tensor(out=e_rest, in0=e_hot1, scalar=NEG, in1=e_val, op0=ALU.mult, op1=ALU.add))
                step(v.tensor_reduce(e_next, e_rest, AX, ALU.max))
                v.tensor_tensor(gap, e_next, e_top, ALU.subtract).then_inc(pair_shift, 1)
                first_of(e_rest, e_next, e_hot2, rank, best)
                for k, e_hot in enumerate((e_hot1, e_hot2)):
                    step.mark(v.tensor_tensor(pick[:, k].rearrange("p t (g e) -> p t g e", g=GROUPS),
                                              g_hot.unsqueeze(3).to_broadcast([P, TILES, 8, 8]),
                                              e_hot.unsqueeze(2).to_broadcast([P, TILES, 8, 8]), ALU.mult))
                step.join()
                v.tensor_tensor(pick[:, 2], pick[:, 0], pick[:, 1], ALU.add).then_inc(picks_ready, 1)
                dve.wait_ge(group_exp, l + 1)
                step(v.tensor_reduce(g_sum, r8[:, 1], AX, ALU.add))
                dve.wait_ge(pair_exp, l + 1)
                step(v.tensor_scalar(share, ratio, 1.0, None, ALU.add))
                step(v.tensor_tensor(share, share, g_sum, ALU.mult))
                step(v.reciprocal(wt[:, 0], share))
                step(v.tensor_tensor(wt[:, 1], wt[:, 0], ratio, ALU.mult))
                dve.wait_ge(counted, l + 1)
                total, upto, start, blocks, b_upto, b_from = (count[:, i] for i in range(6))
                step(v.tensor_copy(total, ps[:, 6, 0:EXPERTS]))
                step(v.tensor_tensor_scan(upto, ones[:, 0:EXPERTS], total, 0.0, ALU.mult, ALU.add))
                step(v.tensor_tensor(start, upto, total, ALU.subtract))
                step(v.tensor_tensor(place[:, :, :], ps[:, 5, 0:TILES * EXPERTS].rearrange("p (t e) -> p t e", t=TILES),
                                     start.unsqueeze(1).to_broadcast([P, TILES, EXPERTS]), ALU.add))
                for k in range(TOPK):
                    step(v.tensor_tensor(placed[:, :, :], pick[:, k], place[:, :, :], ALU.mult))
                    step(v.tensor_reduce(pos[:, k], placed[:, :, :], AX, ALU.add))
                v.tensor_copy(pos_u[:, :], pos[:, :, :].rearrange("p k t -> p (k t)")).then_inc(pos_ready, 1)
                step.mark(v.memset(start_i[0:1, l, EXPERTS:EXPERTS + 2], 0))
                step.mark(v.tensor_copy(start_i[0:1, l, 0:EXPERTS], start[0:1, :]))
                step.mark(v.tensor_copy(count_i[0:1, l, :], total[0:1, :]))
                step(v.tensor_scalar(placed[:, 0, :], total, block_token[:, 0:1], float(4 * ROWS), ALU.is_le, ALU.mult))
                step(v.scalar_tensor_tensor(out=placed[:, 1, :], in0=start, scalar=2.0, in1=placed[:, 0, :], op0=ALU.mult, op1=ALU.add))
                step.mark(v.tensor_scalar(row_of[:, :], placed[:, 1, :], block_half[:, 0:1], None, ALU.add))
                step(v.memset(blocks, 0.0))
                for j in range(1, S // BLOCK):
                    step(v.scalar_tensor_tensor(out=blocks, in0=total, scalar=float(j * BLOCK), in1=blocks,
                                                op0=ALU.is_gt, op1=ALU.add))
                step(v.tensor_tensor_scan(b_upto, ones[:, 0:EXPERTS], blocks, 0.0, ALU.mult, ALU.add))
                step.mark(v.tensor_copy(extra_n[0:1, l:l + 1], b_upto[0:1, EXPERTS - 1:EXPERTS]))
                step(v.tensor_tensor(b_from, b_upto, blocks, ALU.subtract))
                mine, after, row = placed[:, 0, :], placed[:, 1, :], placed[:, 2, :]
                step(v.tensor_scalar(mine, b_from, part_no[:, 0:1], None, ALU.is_le))
                step(v.tensor_scalar(after, b_upto, part_no[:, 0:1], None, ALU.is_gt))
                step(v.tensor_tensor(mine, mine, after, ALU.mult))
                step(v.scalar_tensor_tensor(out=row, in0=b_from, scalar=float(-BLOCK), in1=start, op0=ALU.mult, op1=ALU.add))
                step(v.tensor_scalar(after, part_no[:, 0:1].to_broadcast([P, EXPERTS]), float(BLOCK), float(BLOCK), ALU.mult, ALU.add))
                step(v.tensor_tensor(row, row, after, ALU.add))
                step(v.scalar_tensor_tensor(out=row, in0=upto, scalar=float(-BLOCK), in1=row, op0=ALU.add, op1=ALU.min))
                step(v.tensor_tensor(row, row, mine, ALU.mult))
                step(v.tensor_reduce(extra_f[:, 1:2], row, AX, ALU.add))
                step(v.tensor_tensor(row, mine, expert_no[:, :], ALU.mult))
                step(v.tensor_reduce(extra_f[:, 0:1], row, AX, ALU.add))
                v.tensor_copy(extra_i[:, :], extra_f[:, 0:2]).then_inc(tables_ready, 1)

            def moe_dve(l):
                if 2 * l not in stages:
                    norm()
                route(l)
                for c in range(CHUNKS):
                    dve.wait_ge(chunk_turned, l * CHUNKS + c + 1)
                    nc.vector.tensor_copy(xsT[:, 4:8, c * P:(c + 1) * P],
                                          ps[:, 2 * (c % 2) + 1, :].rearrange("p (k n) -> p k n", k=4)).then_inc(xsT_dve, 1)

                def take_block(where, buffer):
                    return nc.vector.tensor_copy(x_block[:, buffer], xsT[:, :, bass.ds(where, BLOCK)])

                base = l * EXPERTS
                dve.wait_ge(tables_ready, l + 1)
                dve.wait_ge(xsT_act, (l + 1) * CHUNKS)
                dve.wait_ge(xsT_dve, (l + 1) * CHUNKS)
                for n in range(2):
                    r = dve.value_load(start_i[0:1, l, n:n + 1], min_val=0, max_val=ROWS)
                    take_block(r, n).then_inc(block_ready, 1)

                def one_expert(i, u):
                    dve.wait_ge(silu_done, i * 2 + (base + u + 1))
                    nc.vector.tensor_tensor(hid[:, :], silu[:, :], ps[:, UP_BANKS[u], P:2 * P], ALU.mult).then_inc(hid_done, 1)
                    r = dve.value_load(start_i[0:1, l, bass.ds(i * 2 + (u + 2), 1)], min_val=0, max_val=ROWS)
                    take_block(r, u).then_inc(block_ready, 1)
                    dve.wait_ge(down_done, i * 2 + (base + u + 1))
                    if l > 0 or not isinstance(i, int):
                        dve.wait_ge(y_written[u], i * 16 + 16 * (EXPERTS // 2) * l)
                    nc.vector.tensor_copy(row_now[:, u:u + 1], row_of[:, bass.ds(i * 2 + u, 1)])
                    nc.vector.tensor_copy(y_sb[:, u, :], ps[:, 2, :]).then_inc(y_ready, 1)

                for u in range(2):
                    one_expert(0, u)
                with dve.Fori(1, EXPERTS // 2) as i:
                    for u in range(2):
                        one_expert(i, u)
                s = ex[l]
                n = dve.value_load(extra_n[0:1, l:l + 1], min_val=0, max_val=MAX_EXTRA)
                with dve.If(n > 0):
                    for u in range(2):
                        dve.wait_ge(y_written[u], 8 * (base + EXPERTS))
                    dve.wait_ge(extra_made, 16 * 2 * (l + 1))
                    dve.wait_ge(block_ready, (EXPERTS + 2) * (l + 1))
                    with dve.Fori(0, n) as q:
                        r = dve.value_load(extra_t[0:1, l, 1, bass.ds(q, 1)], min_val=0, max_val=ROWS)
                        take_block(r, 0).then_inc(s["block"], 1)
                        dve.wait_ge(s["silu"], q + 1)
                        nc.vector.tensor_tensor(hid[:, :], silu[:, :], ps[:, 0, P:2 * P], ALU.mult).then_inc(s["hid"], 1)
                        dve.wait_ge(s["down"], q + 2)
                        nc.vector.tensor_copy(y_sb[:, 0, :], ps[:, 2, :]).then_inc(s["y"], 1)
                for t in range(TILES):
                    for k in range(TOPK):
                        c = k * TILES + t
                        dve.wait_ge(gathered[c], 16 * (l + 1))
                        add = nc.vector.scalar_tensor_tensor(out=x[:, t, :], in0=y_in[:, c, :], scalar=wt[:, k, t:t + 1],
                                                             in1=x[:, t, :], op0=ALU.mult, op1=ALU.add)
                        if k < TOPK - 1:
                            step(add)
                    add.then_inc(x_ready, 1)

            def attend_dve(first, head0, steps, add_head, between, lead=None):
                def top(s):
                    t, bank = s % TILES, SCORE_BANKS[s % 3]
                    dve.wait_ge(scores_done, first + (s + 1))
                    step(nc.vector.tensor_tensor(ps[:, bank, t * P:(t + 1) * P], ps[:, bank, t * P:(t + 1) * P],
                                                 tri[:, :], ALU.add))
                    nc.vector.tensor_reduce(row_max[:, s % 8:s % 8 + 1], ps[:, bank, 0:(t + 1) * P], AX, ALU.max,
                                            negate=True).then_inc(max_done, 1)

                def finish(j):
                    dve.wait_ge(exp_done, first + (j + 1) * TILES)
                    step(nc.vector.reciprocal(row_inv[:, :], row_sum[:, j % 2 * TILES:(j % 2 + 1) * TILES]))
                    dve.wait_ge(pv_done, head0 + (j + 1))
                    add_head(j)

                for s in range(3):
                    top(s)
                    if s == 0 and lead:
                        lead()
                for s in range(steps + 1):
                    if s + 3 < steps:
                        top(s + 3)
                    if s >= TILES and s % TILES == 0:
                        finish(s // TILES - 1)
                    if s in between:
                        between[s]()

            def add_output(layer):
                m, n = turns[0], mixers[0]
                turns[0] += 1
                mixers[0] += 1
                for t in range(TILES):
                    turned_half(m, t)
                following = 2 * layer + 1 in stages
                norm_no, turn_no = norms[0], turns[0]
                norms[0] += following
                turns[0] += following
                for t in range(TILES):
                    for half in range(2):
                        part = 2 * t + half
                        dve.wait_ge(out_done, n * OUT_PARTS + part + 1)
                        nc.vector.tensor_tensor(x[:, t, half * 512:(half + 1) * 512], x[:, t, half * 512:(half + 1) * 512],
                                                ps[:, 4 + part % OUT_BANKS, :], ALU.add).then_inc(out_added, 1)
                        if following and t >= 1 and half == 0:
                            scale(norm_no, t - 1)
                    dve.wait_ge(out_added, n * OUT_PARTS + 2 * t + 2)
                    nc.vector.engine_nop().then_inc(x_ready, 1)
                    if following and t >= 1:
                        turned_half(turn_no, t - 1)
                if following:
                    scale(norm_no, TILES - 1)
                    turned_half(turn_no, TILES - 1)

            mixers = [0]

            def rotate(rows, heads, first, second, to=None):
                v = nc.vector
                half = ROPE // 2

                def table(i, lo, hi):
                    w = turn[:, i, :, lo:hi]
                    return w.unsqueeze(2).to_broadcast([P, TILES, heads, hi - lo]) if heads else w

                def part(r, lo, hi):
                    return r[:, :, :, lo:hi] if heads else r[:, :, lo:hi]

                step.mark(v.tensor_tensor(first, rows, table(0, 0, ROPE), ALU.mult))
                step.mark(v.tensor_tensor(part(second, 0, half), part(rows, half, ROPE), table(1, 0, half), ALU.mult))
                step.mark(v.tensor_tensor(part(second, half, ROPE), part(rows, 0, half), table(1, half, ROPE), ALU.mult))
                step.join()
                return v.tensor_tensor(rows if to is None else to, first, second, ALU.add)

            def mla_dve():
                v = nc.vector
                norm()
                g_lat = mla_gain[:, 0:2 * LORA]
                g_qn = mla_gain[:, 2 * LORA:2 * LORA + NOPE]
                g_qr = mla_gain[:, 2 * LORA + NOPE:2 * LORA + QK]
                g_kn = mla_gain[:, 2 * LORA + QK:2 * LORA + QK + NOPE]
                g_kr = mla_gain[:, 2 * LORA + QK + NOPE:2 * LORA + 2 * QK]
                dve.wait_ge(small_loaded, SMALL)
                step(v.scalar_tensor_tensor(out=g_qn, in0=g_qn, scalar=MLA_SCALE, in1=g_kn, op0=ALU.mult, op1=ALU.mult))
                step(v.tensor_scalar(g_qr, g_qr, MLA_SCALE, None, ALU.mult))
                for t in range(TILES):
                    dve.wait_ge(c_scales, t + 1)
                    for j, (lo, hi) in enumerate(((0, LORA), (LORA, 2 * LORA))):
                        step.mark(v.scalar_tensor_tensor(out=c_rows[:, t % 2, lo:hi], in0=ps[:, 4 + 2 * (t % 2), lo:hi],
                                                         scalar=mean_sq[:, j, t:t + 1], in1=g_lat[:, lo:hi],
                                                         op0=ALU.mult, op1=ALU.mult))
                    step(v.scalar_tensor_tensor(out=kr_rows[:, t, :], in0=ps[:, 5 + 2 * (t % 2), 0:ROPE],
                                                scalar=mean_sq[:, 2, t:t + 1], in1=g_kr, op0=ALU.mult, op1=ALU.mult))
                    v.engine_nop().then_inc(c_ready, 1)
                rotate(kr_rows, 0, rope_a, rope_b).then_inc(kr_staged, 1)
                dve.wait_ge(kr_staged, 1)

                def take(i, u, tiles):
                    for t in tiles:
                        dve.wait_ge(head_done, i * TILES + (t + 1))
                        v.tensor_copy(head[:, t, :], ps[:, 2 + t % 2, 0:QK + NOPE])
                        v.tensor_copy(v_rows[:, u * TILES + t, :], ps[:, 2 + t % 2, QK + NOPE:HEAD_COLS]).then_inc(head_taken, 1)

                def sum_squares(i):
                    dve.wait_ge(sq_done, i + 1)
                    step.mark(v.tensor_reduce(mean_sq[:, 0, :], squares[:, :, 0:NOPE], AX, ALU.add))
                    step.mark(v.tensor_reduce(mean_sq[:, 1, :], squares[:, :, QK:QK + NOPE], AX, ALU.add))
                    step.mark(v.tensor_reduce(mean_sq[:, 2, :], squares[:, :, NOPE:QK], AX, ALU.add))
                    step.join()
                    step(v.tensor_scalar(mean_sq[:, 0:2, :], mean_sq[:, 0:2, :], 1.0 / NOPE, EPS, ALU.mult, ALU.add))
                    v.tensor_scalar(mean_sq[:, 2, :], mean_sq[:, 2, :], 1.0 / ROPE, EPS, ALU.mult, ALU.add).then_inc(ms_ready, 1)

                def stage(i):
                    dve.wait_ge(rs_ready, i + 1)
                    step.mark(v.tensor_tensor(q_rows[:, :, 0:NOPE], head[:, :, 0:NOPE],
                                             mean_sq[:, 0, :].unsqueeze(2).to_broadcast([P, TILES, NOPE]), ALU.mult))
                    step.mark(v.tensor_tensor(q_rows[:, :, NOPE:QK], head[:, :, NOPE:QK],
                                             mean_sq[:, 2, :].unsqueeze(2).to_broadcast([P, TILES, ROPE]), ALU.mult))
                    step.mark(v.tensor_tensor(k_rows, head[:, :, QK:QK + NOPE],
                                             mean_sq[:, 1, :].unsqueeze(2).to_broadcast([P, TILES, NOPE]), ALU.mult))
                    step.join()
                    step(v.tensor_tensor(q_rows, q_rows, mla_gain[:, 2 * LORA:2 * LORA + QK].unsqueeze(1
                                        ).to_broadcast([P, TILES, QK]), ALU.mult))
                    rotate(q_rows[:, :, NOPE:QK], 0, rope_a, rope_b).then_inc(qk_staged, 1)

                def attend_head(i, u, more):
                    dve.wait_ge(qk_turned, i + 1)
                    v.tensor_copy(knT, ps[:, 4, :]).then_inc(qkT_dve, 1)
                    if more:
                        take(i + 1, 1 - u, range(TILES - 1))

                    def add_head(j):
                        v.tensor_tensor(o_rows[:, :, bass.ds(i * VDIM, VDIM)], ps[:, 6, :].rearrange("p (t n) -> p t n", t=TILES),
                                        row_inv[:, :].unsqueeze(2).to_broadcast([P, TILES, VDIM]), ALU.mult).then_inc(o_taken, 1)

                    attend_dve(i * TILES + NSA_UNITS * TILES, i + NSA_UNITS, TILES, add_head,
                               {0: lambda: sum_squares(i + 1), 1: lambda: stage(i + 1)} if more else {},
                               (lambda: take(i + 1, 1 - u, (TILES - 1,))) if more else None)

                take(0, 0, range(TILES))
                sum_squares(0)
                stage(0)
                with dve.Fori(0, HEADS // 2 - 1) as i:
                    step.enter(i, 2 * MLA_STEPS)
                    for u in range(2):
                        attend_head(i * 2 + u, u, True)
                step.leave(HEADS // 2 - 1)
                attend_head(HEADS - 2, 0, True)
                attend_head(HEADS - 1, 1, False)
                dve.wait_ge(o_taken, NSA_UNITS + HEADS + 1)
                for t in range(TILES):
                    v.engine_nop().then_inc(h_ready, 1)
                add_output(1)

            def nsa_dve():
                v = nc.vector
                norm()
                for z in (ks_low[DH:P], ks_high[0:DH], kw_low[DH:P], kw_high[0:DH], v_blocks, k_blocks, hidden):
                    step.mark(v.memset(z, 0.0))
                dve.wait_ge(small_loaded, SMALL)
                step(v.tensor_scalar(nsa_gain[:, 0:SHARE, :], nsa_gain[:, 0:SHARE, :], DH ** -0.5, None, ALU.mult))
                dve.wait_ge(gates_exp, 1)
                step(v.tensor_scalar(gates[:, :, :], gates[:, :, :], 1.0, None, ALU.add))
                step(v.reciprocal(gates[:, :, :], gates[:, :, :]))
                with dve.Fori(0, KV_GROUPS) as i:
                    step.enter(i, NSA_STEPS)
                    for t in range(TILES):
                        dve.wait_ge(group_done, i * TILES + (t + 1))
                        v.tensor_copy(own[:, t, :], ps[:, 4 + 2 * (t % 2):6 + 2 * (t % 2), :].rearrange(
                            "p b n -> p (b n)")[:, 0:GROUP_IN]).then_inc(group_taken, 1)
                    dve.wait_ge(g_squared, i + 1)
                    step(v.tensor_reduce(group_ms[:, :, :], rot_tmp.rearrange("p t (r d) -> p t r d", d=DH), AX, ALU.add))
                    v.tensor_scalar(group_ms[:, :, :], group_ms[:, :, :], EPS, None, ALU.add).then_inc(g_summed, 1)
                    dve.wait_ge(g_scales, i + 1)
                    rows = own[:, :, 0:NORMED].rearrange("p t (r d) -> p t r d", d=DH)
                    step(v.tensor_tensor(rows, rows, group_ms[:, :, :].unsqueeze(3).to_broadcast([P, TILES, SHARE + 2, DH]), ALU.mult))
                    step(v.tensor_tensor(rows, rows, nsa_gain[:, 0:SHARE + 2, :].unsqueeze(1).to_broadcast(
                        [P, TILES, SHARE + 2, DH]), ALU.mult))
                    rotate(rows, SHARE + 2, qk_rot.rearrange("p t (r d) -> p t r d", d=DH),
                           rot_tmp.rearrange("p t (r d) -> p t r d", d=DH),
                           qk_rot.rearrange("p t (r d) -> p t r d", d=DH)).then_inc(g_staged, 1)
                    dve.wait_ge(g_turned, i + 1)
                    v.tensor_copy(q_pair[:, 0, :], ps[:, 6, :]).then_inc(gT_dve, 1)
                    v.tensor_copy(q_pair[:, 1, :], ps[:, 7, :]).then_inc(gT_dve, 1)
                    v.tensor_copy(kw_low[0:DH], ps[DH:P, 0, :]).then_inc(gT_dve, 1)
                    v.tensor_copy(kw_high[DH:P], ps[DH:P, 0, :]).then_inc(gT_dve, 1)
                    dve.wait_ge(gT_act, i * 6 + 6)
                    v.tensor_copy(kcv_pair[0:DH, 1, :], ps[DH:P, 1, :]).then_inc(gT_dve, 1)
                    v.tensor_copy(kcv_pair[DH:P, 1, 0:S - 1], ps[DH:P, 1, 1:S]).then_inc(gT_dve, 1)

                    def sum_keys():
                        dve.wait_ge(cmp_made, i + 1)
                        dve.wait_ge(vc_ready, i + 1)
                        step(v.tensor_copy(k_cmp[:, 0, :], ps[:, 5, DH:2 * DH]))
                        step(v.tensor_tensor(k_cmp[:, 1, :], k_cmp[:, 0, :], k_cmp[:, 0, :], ALU.mult))
                        step(v.tensor_reduce(kc_ms[:, :], k_cmp[:, 1, :], AX, ALU.add))
                        v.tensor_scalar(kc_ms[:, :], kc_ms[:, :], 1.0 / DH, EPS, ALU.mult, ALU.add).then_inc(kc_summed, 1)

                    def scale_keys():
                        dve.wait_ge(kc_scale, i + 1)
                        step(v.scalar_tensor_tensor(out=k_cmp[:, 0, :], in0=k_cmp[:, 0, :], scalar=kc_ms[:, 0:1],
                                                    in1=nsa_gain[:, SHARE + 2, :], op0=ALU.mult, op1=ALU.mult))
                        v.tensor_copy(k_cmp[:, 1, :], k_cmp[:, 0, :]).then_inc(kc_staged, 1)

                    def place_keys():
                        dve.wait_ge(kc_turned, i + 1)
                        v.tensor_copy(k_blocks[0:DH, 0:CMP_SLOTS], ps[0:DH, 5, 3 * P:3 * P + CMP_SLOTS])
                        v.tensor_copy(k_blocks[DH:P, CMP_SLOTS:2 * CMP_SLOTS], ps[DH:P, 5, 3 * P:3 * P + CMP_SLOTS]).then_inc(kc_ready, 1)

                    bc = [P, TILES, SHARE, CMP_SLOTS]
                    c_sum3 = c_sum[:, :].rearrange("p (t r) -> p t r", t=TILES)

                    def cmp_top():
                        dve.wait_ge(c_scored, i + 1)
                        step(v.tensor_tensor(cmp_p4, ps[:, 5, :].rearrange("p (t r n) -> p t r n", t=TILES, r=SHARE),
                                             cmp_mask[:, 0].unsqueeze(2).to_broadcast(bc), ALU.add))
                        step(v.tensor_reduce(c_max[:, :], cmp_probs, AX, ALU.max))
                        v.tensor_tensor(cmp_probs, cmp_probs, c_max[:, :].unsqueeze(2).to_broadcast([P, TILES * SHARE, CMP_SLOTS]),
                                        ALU.subtract).then_inc(c_shifted, 1)

                    def cmp_masked():
                        dve.wait_ge(c_exp, i + 1)
                        v.tensor_tensor(cmp_p4, cmp_p4, cmp_mask[:, 1].unsqueeze(2).to_broadcast(bc), ALU.mult).then_inc(c_probs, 1)
                        dve.wait_ge(c_probs, i + 1)
                        step(v.tensor_reduce(c_sum[:, :], cmp_probs, AX, ALU.add))
                        step(v.tensor_scalar(c_sum[:, :], c_sum[:, :], 1e-30, None, ALU.max))
                        step(v.reciprocal(c_sum[:, :], c_sum[:, :]))
                        step(v.tensor_tensor(c_sum3, c_sum3, gates[:, :, bass.ds(i * SHARE, SHARE)], ALU.mult))

                    def cmp_take(half):
                        dve.wait_ge(c_weighed, i * 2 + (half + 1))
                        v.tensor_tensor(cmp_out[:, 2 * half:2 * half + 2], ps[:, 5, :].rearrange("p (t r d) -> p t r d", t=2, r=SHARE),
                                        c_sum3[:, 2 * half:2 * half + 2].unsqueeze(3).to_broadcast([P, 2, SHARE, DH]),
                                        ALU.mult).then_inc(c_added, 1) if half == 0 else step(
                            v.tensor_tensor(cmp_out[:, 2 * half:2 * half + 2], ps[:, 5, :].rearrange("p (t r d) -> p t r d", t=2, r=SHARE),
                                            c_sum3[:, 2 * half:2 * half + 2].unsqueeze(3).to_broadcast([P, 2, SHARE, DH]), ALU.mult))

                    between = {AT_MADE + 1: sum_keys, AT_KEYS - 1: scale_keys, AT_KEYS + 1: place_keys, AT_SOFT: cmp_top,
                               AT_SOFT + 2: cmp_masked, AT_WEIGH + 1: lambda: cmp_take(0), AT_WEIGH + 3: lambda: cmp_take(1)}

                    def add_head(j):
                        r, kind = j // 2, j % 2
                        step(v.tensor_tensor(weight[:, :].unsqueeze(2), row_inv[:, :].unsqueeze(2),
                                             gates[:, :, bass.ds(i * SHARE + ((1 + kind) * NSA_HEADS + r), 1)], ALU.mult))
                        dve.wait_ge(o_taken, i * UNITS + (j + 1))
                        for t in range(TILES):
                            cols = o_rows[:, t, bass.ds(i * Q_COLS + r * DH, DH)]
                            got = ps[:, 6 + j % 2, t * DH:(t + 1) * DH]
                            if kind:
                                last = v.scalar_tensor_tensor(out=cols, in0=got, scalar=weight[:, t:t + 1], in1=cols,
                                                              op0=ALU.mult, op1=ALU.add)
                            else:
                                last = v.tensor_scalar(cols, got, weight[:, t:t + 1], None, ALU.mult)
                        last.then_inc(o_taken, 1)

                    attend_dve(i * STEPS, i * UNITS, STEPS, add_head, between)
                    dve.wait_ge(o_taken, i * UNITS + (UNITS + 1))
                    cols = o_rows[:, :, bass.ds(i * Q_COLS, Q_COLS)].rearrange("p t (r d) -> p t r d", r=SHARE)
                    step(v.tensor_tensor(cols, cols, cmp_out, ALU.add))
                step.leave(KV_GROUPS)
                dve.wait_ge(o_taken, KV_GROUPS * UNITS + 1)
                for t in range(TILES):
                    v.engine_nop().then_inc(h_ready, 1)
                add_output(0)

            for ph in range(PHASES):
                if ph in stages:
                    if ph == 0:
                        nsa_dve()
                    if ph == 2:
                        mla_dve()
                    if ph % 2 == 1:
                        moe_dve(ph // 2)


def layout(inputs):
    arrays = {}
    for name, value in inputs.items():
        v = np.asarray(value)
        if name == "x":
            arrays[name] = v[0]
        elif name in ("moe_w_group", "moe_b_group"):
            both = (v, np.asarray(inputs[name.replace("group", "expert")]))
            arrays[name.replace("group", "router")] = np.concatenate(both, axis=-1)
        elif name in ("moe_w_expert", "moe_b_expert"):
            continue
        elif name in ("norm_mix", "norm_ffn") or name.startswith("moe_"):
            arrays[name] = v
        elif name == "nsa_w_in":
            w = v[0].reshape(P, KD, -1)
            q = w[:, :, 0:D].reshape(P, KD, KV_GROUPS, Q_COLS)
            kv = w[:, :, D:D + 6 * KV_GROUPS * DH].reshape(P, KD, 6, KV_GROUPS, DH)
            order = [q] + [kv[:, :, i] for i in (2, 4, 0, 1, 3, 5)]
            arrays["nsa_w_group"] = np.concatenate(order, axis=3).transpose(2, 0, 1, 3)
            arrays["nsa_w_gates"] = w[:, :, D + 6 * KV_GROUPS * DH:]
        elif name == "nsa_cmp_w1":
            arrays[name] = v[0].reshape(2, CMP_LEN // 2, 2, DH, CMP_HIDDEN).transpose(2, 3, 0, 1, 4).reshape(
                P, 2, CMP_LEN // 2, CMP_HIDDEN)
        elif name == "nsa_cmp_pos":
            arrays[name] = v[0].reshape(2, CMP_LEN // 2, 2, DH).transpose(2, 3, 0, 1).reshape(P, 2, CMP_LEN // 2)
        elif name == "nsa_cmp_w2":
            arrays[name] = v[0].transpose(1, 0, 2)
        elif name == "nsa_k_norm":
            for i in range(3):
                arrays[f"nsa_k_norm_{i}"] = v[0, i:i + 1]
        elif name == "nsa_q_norm":
            arrays[name] = v
        elif name == "nsa_w_out":
            arrays[name] = v[0]
        elif name.startswith("mla_w"):
            arrays[name] = v[0]
        elif name.startswith("mla_"):
            arrays[name] = v
    inv = (1.0 / (np.float32(10000.0) ** (np.arange(0, ROPE, 2, dtype=np.float32) / np.float32(ROPE)))).astype(np.float32)
    angle = np.arange(S, dtype=np.float32)[:, None] * inv[None, :]
    cos, sin = np.cos(angle), np.sin(angle)
    rope = np.stack([np.concatenate([cos, cos], 1), np.concatenate([-sin, sin], 1)]).astype(np.float32)
    arrays["rope"] = rope.reshape(2, TILES, P, ROPE).transpose(2, 0, 1, 3)
    ends = np.arange(CMP_SLOTS) * CMP_STRIDE + CMP_LEN - 1
    seen = (ends[None, :] <= np.arange(S)[:, None]) & (np.arange(CMP_SLOTS)[None, :] < N_CMP)
    mask = np.stack([np.where(seen, 0.0, NEG), seen]).astype(np.float32)
    arrays["cmp_mask"] = mask.reshape(2, TILES, P, CMP_SLOTS).transpose(2, 0, 1, 3)
    return {n: np.ascontiguousarray(v) for n, v in arrays.items()}


def kernel(**inputs):
    import concourse.bacc as bacc
    from concourse.bass_utils import run_bass_kernel_spmd

    nc = bacc.Bacc("TRN2", target_bir_lowering=False, num_devices=1)
    arrays = layout(inputs)
    aps = {n: nc.dram_tensor(n, v.shape, mybir.dt.from_np(v.dtype), kind="ExternalInput").ap() for n, v in arrays.items()}
    out = nc.dram_tensor("result", (S, D), F32, kind="ExternalOutput").ap()
    build(nc, aps, out, [0, 1, 2, 3])
    r = run_bass_kernel_spmd(nc, [arrays], core_ids=[0])
    return r.results[0]["result"].reshape(1, S, D)
```
